# Optimizing a Trainium2 kernel written in Bass

```python
import jax, jax.numpy as jnp
from jax import lax
import numpy as np

D_MODEL = 1024
BATCH = 1
SEQ = 1024
DEPTH = 2
DEC_BATCH = 8
DEC_SEQ = 1
PAST_LEN = 2048
PAGE_SIZE = 128

N_MIXERS = 2
N_ATTN_LAYERS = (DEPTH + 1) // 2
N_CONV_LAYERS = DEPTH // 2
N_HEADS = 16
HEAD_DIM = D_MODEL // N_HEADS
CONV_WIDTH = 3
D_FF = -(-8 * D_MODEL // (3 * 256)) * 256
Q_BLOCK = 128
RMS_EPS = 1e-6
FORGET_BIAS_INIT = 3.0
NEG_INF = -1e30

kernel_name = "fox_shortconv_hybrid_step"

def rmsnorm(x, g):
    xf = x.astype(jnp.float32)
    y = xf * lax.rsqrt(jnp.mean(xf * xf, axis=-1, keepdims=True) + RMS_EPS)
    return (y * g.astype(jnp.float32)).astype(x.dtype)

def swiglu(x, w_in, w_out):
    g, u = jnp.split(x @ w_in, 2, axis=-1)
    return (jax.nn.silu(g) * u) @ w_out

def fox_project(h, w_qkvf, b_f):
    B, T, _ = h.shape
    proj = h @ w_qkvf
    q, k, v, f = jnp.split(proj, [D_MODEL, 2 * D_MODEL, 3 * D_MODEL], axis=-1)
    q = q.reshape(B, T, N_HEADS, HEAD_DIM)
    k = k.reshape(B, T, N_HEADS, HEAD_DIM)
    v = v.reshape(B, T, N_HEADS, HEAD_DIM)
    logf = jax.nn.log_sigmoid((f + b_f).astype(jnp.float32))
    return q, k, v, logf

def fox_attend(q, cum_q, q_pos, k, v, cum_kT, k_pos):
    s = jnp.einsum('bqhd,bkhd->bhqk', q, k).astype(jnp.float32) * (HEAD_DIM ** -0.5)
    s = s + jnp.transpose(cum_q, (0, 2, 1))[..., None] - cum_kT[:, :, None, :]
    mask = k_pos[None, :] <= q_pos[:, None]
    s = jnp.where(mask[None, None], s, NEG_INF)
    p = jax.nn.softmax(s, axis=-1)
    return jnp.einsum('bhqk,bkhd->bqhd', p.astype(v.dtype), v)

def fox_prompt(q, k, v, logf):
    B, S, H, Dh = q.shape
    cum = jnp.cumsum(logf, axis=1)
    cum_kT = jnp.transpose(cum, (0, 2, 1))
    nb = S // Q_BLOCK
    qb = jnp.transpose(q.reshape(B, nb, Q_BLOCK, H, Dh), (1, 0, 2, 3, 4))
    cb = jnp.transpose(cum.reshape(B, nb, Q_BLOCK, H), (1, 0, 2, 3))
    starts = jnp.arange(nb, dtype=jnp.int32) * Q_BLOCK
    k_pos = jnp.arange(S, dtype=jnp.int32)

    def block(args):
        q_i, c_i, s0 = args
        q_pos = s0 + jnp.arange(Q_BLOCK, dtype=jnp.int32)
        return fox_attend(q_i, c_i, q_pos, k, v, cum_kT, k_pos)

    o = lax.map(block, (qb, cb, starts))
    return jnp.transpose(o, (1, 0, 2, 3, 4)).reshape(B, S, H * Dh)

def fox_sample(q, k, v, logf, ck, cv, clogf, page_table):
    DB, T, H, Dh = q.shape
    n_pages = page_table.shape[1]
    past = n_pages * PAGE_SIZE
    k_past = ck[page_table].reshape(DB, past, H, Dh)
    v_past = cv[page_table].reshape(DB, past, H, Dh)
    lf_past = clogf[page_table].reshape(DB, past, H).astype(jnp.float32)
    cum_past = jnp.cumsum(lf_past, axis=1)
    cum_new = cum_past[:, -1:] + jnp.cumsum(logf, axis=1)
    k_all = jnp.concatenate([k_past, k.astype(k_past.dtype)], axis=1)
    v_all = jnp.concatenate([v_past, v.astype(v_past.dtype)], axis=1)
    cum_kT = jnp.transpose(jnp.concatenate([cum_past, cum_new], axis=1), (0, 2, 1))
    q_pos = past + jnp.arange(T, dtype=jnp.int32)
    k_pos = jnp.arange(past + T, dtype=jnp.int32)
    o = fox_attend(q, cum_new, q_pos, k_all, v_all, cum_kT, k_pos)
    return o.reshape(DB, T, H * Dh)

def short_conv_mixer(h, prev, w_in, conv_k, w_out):
    T = h.shape[1]
    b, c, u = jnp.split(h @ w_in, 3, axis=-1)
    cu = c * u
    buf = jnp.concatenate([prev.astype(cu.dtype), cu], axis=1)
    y = conv_k[0] * buf[:, 0:T]
    for j in range(1, CONV_WIDTH):
        y = y + conv_k[j] * buf[:, j:j + T]
    return (b * y) @ w_out, buf[:, -(CONV_WIDTH - 1):]

def setup_inputs(seed: int = 0) -> dict:
    key = jax.random.key(seed)
    ks = jax.random.split(key, 24)
    n_pages = PAST_LEN // PAGE_SIZE
    n_used = DEC_BATCH * n_pages
    n_pool = n_used + (n_used + 3) // 4
    f32 = jnp.float32
    nrm = lambda k, shape, scale: jax.random.normal(k, shape, f32) * scale
    page_table = jax.random.permutation(ks[6], n_pool)[:n_used].reshape(DEC_BATCH, n_pages).astype(jnp.int32)
    return {
        "x_prompt": nrm(ks[0], (BATCH, SEQ, D_MODEL), 1.0),
        "x_sample": nrm(ks[1], (DEC_BATCH, DEC_SEQ, D_MODEL), 1.0),
        "cache_k": nrm(ks[2], (N_ATTN_LAYERS, n_pool, PAGE_SIZE, N_HEADS, HEAD_DIM), 1.0),
        "cache_v": nrm(ks[3], (N_ATTN_LAYERS, n_pool, PAGE_SIZE, N_HEADS, HEAD_DIM), 1.0),
        "cache_logf": jax.nn.log_sigmoid(FORGET_BIAS_INIT + nrm(ks[4], (N_ATTN_LAYERS, n_pool, PAGE_SIZE, N_HEADS), 1.0)),
        "state_conv": nrm(ks[5], (N_CONV_LAYERS, DEC_BATCH, CONV_WIDTH - 1, D_MODEL), 1.0),
        "page_table": page_table,
        "norm_mix": 1.0 + nrm(ks[7], (DEPTH, D_MODEL), 0.02),
        "norm_ffn": 1.0 + nrm(ks[8], (DEPTH, D_MODEL), 0.02),
        "w_ffn_in": nrm(ks[9], (DEPTH, D_MODEL, 2 * D_FF), D_MODEL ** -0.5),
        "w_ffn_out": nrm(ks[10], (DEPTH, D_FF, D_MODEL), D_FF ** -0.5),
        "norm_final": 1.0 + nrm(ks[11], (D_MODEL,), 0.02),
        "attn_w_qkvf": nrm(ks[12], (N_ATTN_LAYERS, D_MODEL, 3 * D_MODEL + N_HEADS), D_MODEL ** -0.5),
        "attn_b_f": FORGET_BIAS_INIT + nrm(ks[13], (N_ATTN_LAYERS, N_HEADS), 0.1),
        "attn_w_o": nrm(ks[14], (N_ATTN_LAYERS, D_MODEL, D_MODEL), D_MODEL ** -0.5),
        "conv_w_in": nrm(ks[15], (N_CONV_LAYERS, D_MODEL, 3 * D_MODEL), D_MODEL ** -0.5),
        "conv_kernel": nrm(ks[16], (N_CONV_LAYERS, CONV_WIDTH, D_MODEL), CONV_WIDTH ** -0.5),
        "conv_w_out": nrm(ks[17], (N_CONV_LAYERS, D_MODEL, D_MODEL), D_MODEL ** -0.5),
    }

def reference(x_prompt, x_sample, cache_k, cache_v, cache_logf, state_conv, page_table,
              norm_mix, norm_ffn, w_ffn_in, w_ffn_out, norm_final,
              attn_w_qkvf, attn_b_f, attn_w_o, conv_w_in, conv_kernel, conv_w_out):
    yp, ys = x_prompt, x_sample
    kp_l, vp_l, lp_l, ks_l, vs_l, ls_l, cp_l, cs_l = [], [], [], [], [], [], [], []
    for i in range(DEPTH):
        hp = rmsnorm(yp, norm_mix[i])
        hs = rmsnorm(ys, norm_mix[i])
        li = i // N_MIXERS
        if i % N_MIXERS == 0:
            qp, kp, vp, lfp = fox_project(hp, attn_w_qkvf[li], attn_b_f[li])
            qs, ks_, vs_, lfs = fox_project(hs, attn_w_qkvf[li], attn_b_f[li])
            mp = fox_prompt(qp, kp, vp, lfp) @ attn_w_o[li]
            ms = fox_sample(qs, ks_, vs_, lfs, cache_k[li], cache_v[li], cache_logf[li], page_table) @ attn_w_o[li]
            kp_l.append(kp); vp_l.append(vp); lp_l.append(lfp)
            ks_l.append(ks_); vs_l.append(vs_); ls_l.append(lfs)
        else:
            zeros_prev = jnp.zeros((yp.shape[0], CONV_WIDTH - 1, D_MODEL), yp.dtype)
            mp, cpn = short_conv_mixer(hp, zeros_prev, conv_w_in[li], conv_kernel[li], conv_w_out[li])
            ms, csn = short_conv_mixer(hs, state_conv[li], conv_w_in[li], conv_kernel[li], conv_w_out[li])
            cp_l.append(cpn); cs_l.append(csn)
        yp = yp + mp
        ys = ys + ms
        yp = yp + swiglu(rmsnorm(yp, norm_ffn[i]), w_ffn_in[i], w_ffn_out[i])
        ys = ys + swiglu(rmsnorm(ys, norm_ffn[i]), w_ffn_in[i], w_ffn_out[i])
    y_prompt = rmsnorm(yp, norm_final)
    y_sample = rmsnorm(ys, norm_final)
    return (y_prompt, y_sample,
            jnp.stack(kp_l), jnp.stack(vp_l), jnp.stack(lp_l),
            jnp.stack(ks_l), jnp.stack(vs_l), jnp.stack(ls_l),
            jnp.stack(cp_l), jnp.stack(cs_l))


_drawn_inputs = setup_inputs


def setup_inputs(seed=0):
    import zlib

    import numpy as np

    out = dict(_drawn_inputs(seed))
    spreads = {}
    factors = {}
    for name, (base, spread) in spreads.items():
        noise = np.random.default_rng([zlib.crc32(name.encode()), seed]).standard_normal(out[name].shape)
        drawn = base * np.exp(spread * noise) if base else spread * noise
        out[name] = __import__('jax').numpy.asarray(drawn.astype(out[name].dtype))
    for name, factor in factors.items():
        out[name] = (out[name] * factor).astype(out[name].dtype)
    return out
```

```python
from contextlib import ExitStack, contextmanager

import concourse.bass as bass
from concourse import mybir

F32 = mybir.dt.float32
F32R = mybir.dt.float32r
BF16 = mybir.dt.bfloat16
I32 = mybir.dt.int32
ALU = mybir.AluOpType
ACT = mybir.ActivationFunctionType
X_AXIS = mybir.AxisListType.X

P = 128
NEG_INF = -1e30
RMS_EPS = 1e-6


class Count:

    def __init__(self, semaphore, step=1):
        self.sem, self.step, self.value, self.ups = semaphore, step, 0, 0

    def up(self):
        self.value = self.value + self.step
        self.ups += 1
        return self.value


@contextmanager
def counted_loop(engine, start, end, per):
    bases = {c: (c.value, c.ups) for c in per}
    with engine.Fori(start, end) as i:
        for c, n in per.items():
            c.value = (i - start) * (n * c.step) + c.value if start else i * (n * c.step) + c.value
        yield i
    for c, n in per.items():
        value, ups = bases[c]
        assert c.ups - ups == n, (c.sem, c.ups - ups, n)
        c.value = value + (end - start) * n * c.step


def fox_shortconv_hybrid_step(
    nc, x_prompt, x_sample, cache_k, cache_v, cache_logf, state_conv, page_table,
    norm_mix, norm_ffn, w_ffn_in, w_ffn_out, norm_final,
    attn_w_qkvf, attn_b_f, attn_w_o, conv_w_in, conv_kernel, conv_w_out,
    y_prompt, y_sample, k_prompt, v_prompt, logf_prompt,
    k_sample, v_sample, logf_sample, conv_prompt, conv_sample,
):
    _, S, D = x_prompt.shape
    NSEQ = x_sample.shape[0]
    _, POOL, PAGE, H, DH = cache_k.shape
    NPG = page_table.shape[1]
    DFF = w_ffn_out.shape[1]
    T = S + NSEQ
    KT = D // P
    TT = S // P
    NB = 3
    TB = T // NB
    BANK = 512
    NPAIR = H // 2
    QS = DH ** -0.5
    NPAGES = NSEQ * NPG
    KSLOT, VSLOT = 4, 2
    HID = DFF // P
    CHUNKS = [6, 6, 5, 5]
    assert TB * NB == T and TB <= BANK and PAGE == P and NPAIR == NSEQ == KT == TT == 8
    assert DH * 2 == P and NPG == 16 and NPAGES == P and sum(CHUNKS) == HID

    x_tok = x_prompt.rearrange("o (t p) d -> p (o t) d", p=P)
    x_smp = x_sample.rearrange("b o d -> (b o) d")
    k_pages = cache_k.rearrange("l g p h d -> (l g) p (h d)")
    v_pages = cache_v.rearrange("l g p h d -> (l g) p (h d)")
    logf_pages = cache_logf.rearrange("l g p h -> (l g) (p h)")
    w_qkvf = attn_w_qkvf.rearrange("l k n -> (l k) n")
    w_o = attn_w_o.rearrange("l k n -> (l k) n")
    w_cin = conv_w_in.rearrange("l k n -> (l k) n")
    w_cout = conv_w_out.rearrange("l k n -> (l k) n")
    w_in = [w_ffn_in[l, :, :] for l in range(2)]
    w_out = [w_ffn_out[l, :, :] for l in range(2)]
    k_out = k_prompt.rearrange("l o (t p) h d -> p (l o t) (h d)", p=P)
    v_out = v_prompt.rearrange("l o (t p) h d -> p (l o t) (h d)", p=P)
    x_spill = nc.dram_tensor("x_spill", [KT, P, T], F32, kind="Internal").ap()
    o_spill = nc.dram_tensor("o_spill", [KT, P, S], F32, kind="Internal").ap()
    q_spill = nc.dram_tensor("q_spill", [NSEQ, D], F32, kind="Internal").ap()

    def w_tile(w, row, kts, col):
        return w[row:row + kts * P, bass.ds(col, P)].rearrange("(k p) c -> p k c", p=P)

    ctx = ExitStack()
    with ctx:
        def sb(name, shape, dt, stack=ctx):
            return stack.enter_context(nc.sbuf_tensor(name, shape, dt))

        def sem(name):
            return ctx.enter_context(nc.semaphore(name))

        PS = ctx.enter_context(nc.psum_tensor("PS", [P, 8 * BANK], F32))

        def group(s):
            return PS[:, 3 * s * BANK:3 * (s + 1) * BANK].rearrange("p (b n) -> p b n", b=NB)[:, :, 0:TB]

        def bank(n, a=0, b=BANK):
            return PS[:, n * BANK + a:n * BANK + b]

        def blocks(ap):
            return ap.rearrange("p (b n) -> p b n", b=NB)

        RS_TAIL = 5 * BANK + 400

        with ExitStack() as over:
            y_tok = sb("y_tok", [P, TT, D], F32, over)
            y_smp = sb("y_smp", [NSEQ, D], F32, over)
        a_hi = sb("a_hi", [P, KT, T], F32R)
        a_lo = sb("a_lo", [P, KT, T], F32R)
        raw = [sb(f"raw{s}", [P, KT, P], F32) for s in range(2)]
        w_hi = [sb(f"w_hi{s}", [P, KT, P], F32R) for s in range(2)]
        w_lo = [sb(f"w_lo{s}", [P, KT, P], F32R) for s in range(2)]
        rinv = sb("rinv", [P, T], F32)
        ident = sb("ident", [P, P], F32)
        ones = sb("ones", [P, P], F32)
        vecs = sb("vecs", [P, KT, 24], F32)
        o_smp = sb("o_smp", [P, KT, NSEQ], F32)
        eps = sb("eps", [P, 1], F32)

        att = ExitStack()
        s_bias = sb("s_bias", [P, H, NPAGES], F32, att)
        s_new = sb("s_new", [P, NSEQ, H], F32, att)
        negcum = sb("negcum", [P, S], F32R, att)
        v_s = sb("v_s", [NSEQ, D], F32, att)
        ident_b = sb("ident_b", [P, P], BF16, att)
        mask_b = sb("mask_b", [P, P], BF16, att)
        sel_id = sb("sel_id", [P, H], F32, att)
        pages_sb = sb("pages_sb", [1, NPAGES], I32, att)
        with ExitStack() as front:
            xtok = sb("xtok", [P, TT, D], F32, front)
            xsmp = sb("xsmp", [NSEQ, D], F32, front)
            vrow = sb("vrow", [24, D], F32, front)
            xf = [sb(f"xf{s}", [P, T], F32, front) for s in range(2)]
            sqt0 = sb("sqt0", [P, T], F32, front)
            sqs0 = sb("sqs0", [P, T], F32, front)
            hs = sb("hs", [P, KT, NSEQ], F32, front)
            small = sb("small", [P, 8], F32, front)
            bf_col = sb("bf_col", [H, 1], F32, front)
            wseg = [sb(f"wseg{s}", [P, KT, 256], F32, front) for s in range(2)]
            q_s = sb("q_s", [NSEQ, D], F32, front)
            k_s = sb("k_s", [NSEQ, D], F32, front)
            lt = sb("lt", [P, (TT + 1) * H], F32, front)
            page_col = sb("page_col", [P, 1], I32, front)
            suffix = sb("suffix", [P, P], F32, front)
            owner = sb("owner", [NSEQ, P], F32, front)
            tot = sb("tot", [P, H], F32, front)
            snew_row = sb("snew_row", [NSEQ, H], F32, front)
            negd = sb("negd", [NSEQ, NSEQ], F32, front)
            mask_f = sb("mask_f", [P, P], F32, front)
        with ExitStack() as front2:
            lf = sb("lf", [P, PAGE * H], F32, front2)
            lc = sb("lc", [P, PAGE * H], F32, front2)
            gz = sb("gz", [H, T], F32, front2)
            ge = sb("ge", [H, T], F32, front2)
            gw = sb("gw", [H, T], F32, front2)
            gd = sb("gd", [H, T], F32, front2)
        with ExitStack() as loop:
            q_hi = sb("q_hi", [P, S], F32R, loop)
            q_lo = sb("q_lo", [P, S], F32R, loop)
            k_hi = sb("k_hi", [P, S], F32R, loop)
            k_lo = sb("k_lo", [P, S], F32R, loop)
            qv_raw = sb("qv_raw", [P, T], F32, loop)
            k_raw = sb("k_raw", [P, T], F32, loop)
            k_tok = sb("k_tok", [P, TT, P], F32, loop)
            v_tok = sb("v_tok", [P, TT, P], F32, loop)
            v_pack = sb("v_pack", [P, TT, 2, 2, DH], F32R, loop)
            probs = [sb(f"probs{n}", [P, S], F32, loop) for n in range(4)]
            pt_hi = [sb(f"pt_hi{n}", [P, BANK], F32R, loop) for n in range(2)]
            pt_lo = [sb(f"pt_lo{n}", [P, BANK], F32R, loop) for n in range(2)]
            sel = [sb(f"sel{h}", [P, P], F32R, loop) for h in range(2)]
            kpage = sb("kpage", [P, KSLOT, D], F32, loop)
            vpage = sb("vpage", [P, VSLOT, D], F32, loop)
            q_bc = sb("q_bc", [P, D], F32, loop)
            o_pair = sb("o_pair", [P, S], F32, loop)
            o_tmp = sb("o_tmp", [P, 256], F32, loop)
            nmax = sb("nmax", [P, 16], F32, loop)
            lsum = sb("lsum", [P, 16], F32, loop)
            s_raw = sb("s_raw", [P, NPG, H], F32, loop)
            z = sb("z", [P, NPG + 1, H], F32, loop)
            ps = sb("ps", [P, NPG + 1, H], F32, loop)
            zmax = sb("zmax", [P, H], F32, loop)
            mcol = sb("mcol", [H, 1], F32, loop)
            mdiag = sb("mdiag", [H, H], F32, loop)
            psum_s = sb("psum_s", [P, H], F32, loop)
            rl = sb("rl", [P, 1], F32, loop)
            o_rows = sb("o_rows", [P, 256], F32, loop)
        att.close()

        x_res = sb("x_res", [P, KT, T], F32)
        b_hi = sb("b_hi", [P, KT, T], F32R)
        b_lo = sb("b_lo", [P, KT, T], F32R)
        t0 = sb("t0", [P, T], F32)
        t1 = sb("t1", [P, T], F32)
        t2 = sb("t2", [P, T + 2], F32)
        t3 = sb("t3", [P, T], F32)
        conv_rows = sb("conv_rows", [P, KT, 2 + NSEQ], F32)

        w_raw = [sem(f"w_raw{s}") for s in range(2)]
        w_hid = [sem(f"w_hid{s}") for s in range(2)]
        w_lod = [sem(f"w_lod{s}") for s in range(2)]
        mm = [sem(f"mm{s}") for s in range(2)]
        ev = [sem(f"ev{s}") for s in range(2)]
        dv = sem("dv")
        ac = sem("ac")
        po = sem("po")
        cst = sem("cst")
        cst_b = sem("cst_b")
        x_in = sem("x_in")
        vrow_in = sem("vrow_in")
        misc_in = sem("misc_in")
        lf_in = sem("lf_in")
        vec_t = sem("vec_t")
        vec_d = sem("vec_d")
        ftr = sem("ftr")
        fev = sem("fev")
        xsp = [sem(f"xsp{s}") for s in range(2)]
        ahi = sem("ahi")
        alo = sem("alo")
        sqr = sem("sqr")
        sqa = sem("sqa")
        rs = sem("rs")
        rq = sem("rq")
        rr = sem("rr")
        fz = sem("fz")
        fa = sem("fa")
        lgt_in = sem("lgt_in")
        lgt = sem("lgt")
        lgo = sem("lgo")
        out0 = sem("out0")
        rsm = sem("rsm")
        hsd = sem("hsd")
        wsg = [sem(f"wsg{s}") for s in range(2)]
        smm = sem("smm")
        sme = sem("sme")
        qsp = sem("qsp")
        lct = sem("lct")
        lco = sem("lco")
        lcb = sem("lcb")
        lbt = sem("lbt")
        lbe = sem("lbe")
        ready = sem("ready")
        qkv_h = sem("qkv_h")
        qkv_l = sem("qkv_l")
        tkt = sem("tkt")
        tke = sem("tke")
        tkl = sem("tkl")
        ktd = sem("ktd")
        vtd = sem("vtd")
        seld = sem("seld")
        sd = sem("sd")
        mxd = sem("mxd")
        exd = sem("exd")
        pzd = sem("pzd")
        pnd = sem("pnd")
        ptd = sem("ptd")
        pth = sem("pth")
        ptl = sem("ptl")
        pvd = sem("pvd")
        ocp = sem("ocp")
        oad = sem("oad")
        osp = sem("osp")
        kin = [sem(f"kin{n}") for n in range(KSLOT)]
        vin = [sem(f"vin{n}") for n in range(VSLOT)]
        qbi = sem("qbi")
        kml = sem("kml")
        kfr = sem("kfr")
        vfr = sem("vfr")
        sa1 = sem("sa1")
        sa2 = sem("sa2")
        sa3 = sem("sa3")
        sa4 = sem("sa4")
        sa5 = sem("sa5")
        sa6 = sem("sa6")
        sa7 = sem("sa7")
        sa8 = sem("sa8")
        so1 = sem("so1")
        so2 = sem("so2")
        sa9 = sem("sa9")
        oin = [sem(f"oin{s}") for s in range(2)]
        oas = sem("oas")
        bhi = sem("bhi")
        blo = sem("blo")
        xin = sem("xin")
        sil = sem("sil")
        prd = sem("prd")
        cvt = sem("cvt")
        cvp = sem("cvp")
        cvc = sem("cvc")
        yt = sem("yt")
        ytt = sem("ytt")
        yte = sem("yte")
        outs = sem("outs")

        NORMS = dict(mix0=0, mix1=1, ffn0=2, ffn1=3, final=4)
        TAP = 5
        PREV = 8
        steps16 = [(h, t) for h in range(2) for t in range(TT)]
        POOL_K = (1, 3, 5, 7, 9, 11, 12, 13, 14, 15)
        KEYS_IN_PROJECTION = 12
        S_OUT, S_SUM, S_MAX, S_SPREAD = 0, 256, 272, 400
        HQ = H // 4

        def ctr(*sems):
            return [Count(s) for s in sems]

        block = ctx.enter_context(nc.Block())

        @block.sync
        def _(sp):
            sp.dma_start(vrow[0:2, :], norm_mix).then_inc(vrow_in, 16)
            sp.dma_start(vrow[2:4, :], norm_ffn).then_inc(vrow_in, 16)
            sp.dma_start(vrow[4:5, :], norm_final.rearrange("(o d) -> o d", o=1)).then_inc(vrow_in, 16)
            sp.dma_start(vrow[TAP:TAP + 3, :], conv_kernel.rearrange("l j d -> (l j) d")).then_inc(vrow_in, 16)
            sp.dma_start(vrow[PREV:24, :], state_conv.rearrange("l b j d -> (l b j) d")).then_inc(vrow_in, 16)
            sp.dma_start(xsmp[:, :], x_smp).then_inc(x_in, 16)
            sp.dma_start(xtok[:, :, :], x_tok).then_inc(x_in, 16)
            sp.dma_start(pages_sb[:, :], page_table.rearrange("b (o g) -> o (b g)", o=1)).then_inc(misc_in, 16)
            sp.dma_start(page_col[:, :], page_table.rearrange("b (g o) -> (b g) o", o=1)).then_inc(misc_in, 16)
            sp.dma_start(bf_col[:, :], attn_b_f.rearrange("l (h o) -> (l h) o", o=1)).then_inc(misc_in, 16)

            wl = [Count(w_lod[s]) for s in range(2)]

            def load_w(s, src, kts=KT, cols=P, first=False):
                if not first:
                    sp.wait_ge(w_lod[s], wl[s].up())
                sp.dma_start(raw[s][:, 0:kts, 0:cols], src).then_inc(w_raw[s], 16)

            load_w(0, w_qkvf[:, 3 * D:3 * D + H].rearrange("(k p) c -> p k c", p=P), cols=H, first=True)
            load_w(1, w_tile(w_qkvf, 0, KT, D), first=True)
            NSEG = 3 * D // 256
            for n in range(NSEG):
                if n == 2:
                    for m in range(KT):
                        sp.wait_ge(fev, m + 1)
                        sp.dma_start(x_spill[m, :, :], xf[m % 2][:, :]).then_inc(xsp[m % 2], 16)
                    load_w(0, w_tile(w_qkvf, 0, KT, 0))
                if n >= 2:
                    sp.wait_ge(smm, n - 1)
                sp.dma_start(wseg[n % 2][:, :, :],
                             w_qkvf[:, n * 256:(n + 1) * 256].rearrange("(k p) c -> p k c", p=P)).then_inc(wsg[n % 2], 16)
            sp.wait_ge(sme, NSEG)
            sp.dma_start(q_spill, q_s[:, :]).then_inc(qsp, 16)
            sp.dma_start(k_sample.rearrange("l b o h d -> (l b o) (h d)"), k_s[:, :]).then_inc(out0, 16)
            sp.dma_start(v_sample.rearrange("l b o h d -> (l b o) (h d)"), v_s[:, :]).then_inc(out0, 16)
            sp.wait_ge(lgo, 1)
            sp.dma_start(logf_prompt.rearrange("l o (t p) h -> p (l o t) h", p=P),
                         lt[:, 0:TT * H].rearrange("p (t h) -> p t h", h=H)).then_inc(out0, 16)
            sp.dma_start(logf_sample.rearrange("l b o h -> (l b o) h"),
                         lt[0:NSEQ, TT * H:(TT + 1) * H]).then_inc(out0, 16)
            sp.wait_ge(ready, 1)
            sp.wait_ge(out0, 64)
            sp.wait_ge(qsp, 16)
            sp.wait_ge(xsp[0], 16 * KT // 2)
            sp.wait_ge(xsp[1], 16 * KT // 2)
            sp.wait_ge(misc_in, 48)

            kf, vf = ctr(kfr, vfr)

            def page_id(n):
                return sp.value_load(pages_sb[0:1, bass.ds(n, 1)], min_val=0, max_val=POOL - 1)

            def load_k(i, g, fresh):
                if not fresh:
                    sp.wait_ge(kfr, kf.up())
                src = k_pages[bass.ds(page_id(i * NPG + g), 1), :, :].rearrange("a p n -> p (a n)")
                sp.dma_start(kpage[:, g % KSLOT, :], src).then_inc(kin[g % KSLOT], 16)

            def load_v(b, g, fresh):
                if not fresh:
                    sp.wait_ge(vfr, vf.up())
                src = v_pages[bass.ds(page_id(b * NPG + g), 1), :, :].rearrange("a p n -> p (a n)")
                sp.dma_start(vpage[:, g % VSLOT, :], src).then_inc(vin[g % VSLOT], 16)

            def pair(i, first=False, v_fresh=False, last=False):
                if first:
                    sp.dma_start(q_bc[:, :], q_spill[0:1, :].to_broadcast([P, D])).then_inc(qbi, 16)
                load_w(0, w_tile(w_qkvf, 0, KT, i * P + 2 * D))
                if not first:
                    sp.wait_ge(kfr, kf.value + KSLOT)
                    sp.dma_start(q_bc[:, :], q_spill[bass.ds(i, 1), :].to_broadcast([P, D])).then_inc(qbi, 16)
                for g in range(KEYS_IN_PROJECTION):
                    load_k(i, g, first and g < KSLOT)
                for n in range(16):
                    if n % 2 == 0 and n // 2 < NPG - KEYS_IN_PROJECTION:
                        load_k(i, KEYS_IN_PROJECTION + n // 2, False)
                    if not first:
                        load_v(i - 1, n, v_fresh and n < VSLOT)
                    if n == 2:
                        load_w(0, w_tile(w_o, 0, KT, 0) if last else w_tile(w_qkvf, 0, KT, (i + 1) * P))
                        load_w(1, w_tile(w_o, 0, KT, P) if last else w_tile(w_qkvf, 0, KT, (i + 1) * P + D))

            pair(0, first=True)
            pair(1, v_fresh=True)
            with counted_loop(sp, 2, NPAIR - 1, {wl[0]: 2, wl[1]: 1, kf: 16, vf: 16}) as i:
                pair(i)
            pair(NPAIR - 1, last=True)
            for n in range(NPG):
                load_v(NPAIR - 1, n, False)

            sp.wait_ge(osp, 16 * NPAIR)
            sp.wait_ge(sa9, NSEQ)
            sp.wait_ge(ktd, 16 * NPAIR)
            sp.wait_ge(vtd, 16 * NPAIR)
            for m in range(KT):
                if m >= 2:
                    sp.wait_ge(blo, m - 1)
                sp.dma_start((t0, t1)[m % 2][:, 0:S], o_spill[m, :, :]).then_inc(oin[m % 2], 16)
            sp.dma_start(x_res[:, :, :], x_spill.rearrange("k p t -> p k t")).then_inc(xin, 16)

            def out_loads(w, row, kts, first_pair=0):
                with counted_loop(sp, first_pair, KT // 2, {wl[0]: 1, wl[1]: 1}) as i:
                    load_w(0, w_tile(w, row, kts, i * (2 * P)), kts)
                    load_w(1, w_tile(w, row, kts, i * (2 * P) + P), kts)

            def ffn_loads(l):
                h0 = 0
                for n in CHUNKS:
                    with counted_loop(sp, 0, n, {wl[0]: 1, wl[1]: 1}) as j:
                        load_w(0, w_tile(w_in[l], 0, KT, j * P + h0 * P))
                        load_w(1, w_tile(w_in[l], 0, KT, j * P + (h0 * P + DFF)))
                    out_loads(w_out[l], h0 * P, n)
                    h0 += n

            out_loads(w_o, 0, KT, first_pair=1)
            ffn_loads(0)
            with counted_loop(sp, 0, KT // 2, {wl[0]: 3, wl[1]: 3}) as i:
                for m in range(2):
                    for r in range(3):
                        load_w((3 * m + r) % 2, w_tile(w_cin, 0, KT, i * (2 * P) + (m * P + r * D)))
            out_loads(w_cout, 0, KT)
            ffn_loads(1)
            for n in range(TT):
                sp.wait_ge(yte, 2 * KT)
                sp.dma_start(y_prompt.rearrange("o (t p) d -> p (o t) d", p=P)[:, n, :], y_tok[:, n, :]).then_inc(outs, 16)
            sp.dma_start(y_sample.rearrange("b o d -> (b o) d"), y_smp[:, :]).then_inc(outs, 16)
            sp.dma_start(conv_sample[0, :, 0, :], state_conv[0, :, 1, :]).then_inc(outs, 16)
            sp.wait_ge(outs, 16 * (TT + 2 + 2))

        @block.gpsimd
        def _(gp):
            def own(ins, sem_=po):
                ins.then_inc(sem_, 1)

            steps = Count(po)

            def then(ins):
                ins.then_inc(po, 1)
                gp.wait_ge(po, steps.up())

            gp.memset(eps[:, :], RMS_EPS)
            then(gp.memset(ones[:, :], 1.0))
            gp.affine_select(out=ident[:, :], in_=ones[:, :], compare_op=ALU.is_equal, fill=0.0, base=0,
                             pattern=[[-1, P]], channel_multiplier=1).then_inc(cst, 1)
            then(gp.memset(mask_f[:, :], 0.0))
            gp.affine_select(out=mask_f[:, :], in_=mask_f[:, :], compare_op=ALU.is_ge, fill=NEG_INF, base=0,
                             pattern=[[-1, P]], channel_multiplier=1).then_inc(cst, 1)
            then(gp.affine_select(out=suffix[:, :], in_=ones[:, :], compare_op=ALU.is_ge, fill=0.0, base=0,
                                  pattern=[[-1, P]], channel_multiplier=1))
            then(gp.affine_select(out=suffix[:, :], in_=suffix[:, :], compare_op=ALU.is_ge, fill=0.0, base=NPG - 1,
                                  pattern=[[NPG, NSEQ], [0, NPG]], channel_multiplier=-1))
            then(gp.affine_select(out=owner[:, :], in_=ones[0:NSEQ, :], compare_op=ALU.is_ge, fill=0.0, base=0,
                                  pattern=[[1, P]], channel_multiplier=-NPG))
            gp.affine_select(out=owner[:, :], in_=owner[:, :], compare_op=ALU.is_ge, fill=0.0, base=NPG - 1,
                             pattern=[[-1, P]], channel_multiplier=NPG).then_inc(cst, 1)
            then(gp.memset(sel_id[:, :], 0.0))
            for q in range(4):
                ins = gp.affine_select(out=sel_id[:, :], in_=sel_id[:, :], compare_op=ALU.not_equal, fill=1.0,
                                       base=-32 * q, pattern=[[-1, H]], channel_multiplier=1)
                if q < 3:
                    then(ins)
                else:
                    ins.then_inc(cst, 1)
            gp.memset(s_new[:, :, :], NEG_INF).then_inc(cst, 1)
            gp.memset(negcum[:, :].bitcast(F32), 0.0).then_inc(cst, 1)
            gp.memset(w_hi[0][:, :, :].bitcast(F32), 0.0).then_inc(cst, 1)
            gp.wait_ge(misc_in, 48)

            wh = [Count(w_hid[s]) for s in range(2)]
            sq = Count(sqr)

            def low(s, kts=KT, cols=P):
                gp.wait_ge(w_hid[s], wh[s].up())
                gp.tensor_tensor(w_lo[s][:, 0:kts, 0:cols], raw[s][:, 0:kts, 0:cols],
                                 w_hi[s][:, 0:kts, 0:cols].bitcast(F32), ALU.subtract).then_inc(w_lod[s], 1)

            sums = Count(sqa)

            def add_squares(total, tile, first=False):
                gp.wait_ge(sqr, sq.up())
                if not first:
                    gp.wait_ge(sqa, sums.value)
                gp.tensor_tensor(total, total, tile, ALU.add).then_inc(sqa, 1)
                sums.up()

            then(gp.memset(sqs0[:, :], 0.0))
            then(gp.memset(w_lo[0][:, :, :].bitcast(F32), 0.0))
            for m in range(KT):
                add_squares(sqs0[:, :], sqt0[:, :], first=m == 0)
                if m == 0:
                    low(0, cols=H)
                    low(1)
            gp.wait_ge(ftr, KT)
            gp.wait_ge(vec_t, 1)
            gp.indirect_dma_start(out=lf[:, :], out_offset=None, in_=logf_pages,
                                  in_offset=bass.IndirectOffsetOnAxis(ap=page_col[:, 0:1], axis=0)).then_inc(lf_in, 16)
            low(0)
            gp.wait_ge(ready, 1)

            kp = [Count(kin[n], 16) for n in range(KSLOT)]
            qb = Count(qbi, 16)
            npd = Count(ptd)

            def multiply(g):
                kp[g % KSLOT].up()
                if g in POOL_K:
                    gp.wait_ge(kin[g % KSLOT], kp[g % KSLOT].value)
                    gp.tensor_tensor(kpage[:, g % KSLOT, :], kpage[:, g % KSLOT, :], q_bc[:, :], ALU.mult)\
                      .then_inc(kml, 1)

            def zero_block(h, t):
                if t % 2 == 0:
                    c = 128 * (t + 1)
                    gp.tensor_tensor(probs[(4 * h + t // 2) % 2 * 2][:, c:c + P], ones[:, :], ones[:, :],
                                     ALU.subtract).then_inc(pzd, 1)

            gran = [2 * 0 + 1, 2, 3, 4] * 2

            def pair(first):
                gp.wait_ge(qbi, qb.up())
                for g in range(4):
                    multiply(g)
                low(0)
                for g in range(4, KEYS_IN_PROJECTION):
                    multiply(g)
                for n in range(8):
                    h, jj = n // 4, n % 4
                    if n >= 2:
                        for _ in range(gran[n - 2]):
                            npd.up()
                        gp.wait_ge(ptd, npd.value)
                    elif not first:
                        for _ in range(gran[6 + n]):
                            npd.up()
                        gp.wait_ge(ptd, npd.value)
                    zero_block(h, 2 * jj)
                    if n % 2 == 1:
                        multiply(KEYS_IN_PROJECTION + n // 2)
                    if n == 2:
                        low(1)
                    if n == 3:
                        low(0)

            pair(True)
            with counted_loop(gp, 1, NPAIR, {qb: 1, wh[0]: 2, wh[1]: 1, npd: 20,
                                             **{kp[n]: 4 for n in range(KSLOT)}}) as i:
                pair(False)

            z3 = t2[:, 0:T]
            rsc = Count(rs)

            def out_lows(last=False, final=False):
                def turn(more=True):
                    for s in range(2):
                        if more:
                            low(s)
                        if final:
                            add_squares(z3, t3[:, :])
                if final:
                    gp.wait_ge(rs, rsc.up())
                    then(gp.memset(z3, 0.0))
                per = {wh[0]: 1, wh[1]: 1}
                if final:
                    per |= {sq: 2, sums: 2}
                with counted_loop(gp, 0, KT // 2 - (1 if last else 0), per) as i:
                    turn()
                if last:
                    turn(False)

            hi_c = Count(bhi)

            def ffn_lows(last):
                for c, n in enumerate(CHUNKS):
                    with counted_loop(gp, 0, n, {wh[0]: 1, wh[1]: 1, hi_c: 1}) as j:
                        low(0)
                        low(1)
                        gp.wait_ge(bhi, hi_c.up())
                        gp.tensor_tensor(b_lo[:, bass.ds(j, 1), :].rearrange("p a t -> p (a t)"), t1[:, :],
                                         b_hi[:, bass.ds(j, 1), :].rearrange("p a t -> p (a t)").bitcast(F32),
                                         ALU.subtract).then_inc(blo, 1)
                    end = c == len(CHUNKS) - 1
                    out_lows(last=last and end, final=end)

            hi_c.value = KT
            gp.wait_ge(oad, 8 * NPAIR)
            gp.wait_ge(sa9, NSEQ)
            out_lows(final=True)
            ffn_lows(False)
            with counted_loop(gp, 0, KT // 2, {wh[0]: 3, wh[1]: 3}) as i:
                for r in range(6):
                    low(r % 2)
            hi_c.value = hi_c.value + KT
            gp.wait_ge(blo, hi_c.value)
            out_lows(final=True)
            ffn_lows(True)

        @block.scalar
        def _(act):
            wr = [Count(w_raw[s], 16) for s in range(2)]
            done = [Count(mm[s]) for s in range(2)]
            evc = [Count(ev[s]) for s in range(2)]
            steps = Count(ac)

            def then(ins):
                ins.then_inc(ac, 1)
                act.wait_ge(ac, steps.up())

            def high(s, cols=P, fresh=False):
                act.wait_ge(w_raw[s], wr[s].up())
                if not fresh:
                    act.wait_ge(mm[s], done[s].up())
                act.activation(w_hi[s][:, :, 0:cols], raw[s][:, :, 0:cols], ACT.Copy).then_inc(w_hid[s], 1)

            act.wait_ge(x_in, 32)
            act.wait_ge(cst, 7)
            then(act.activation(sqt0[0:NSEQ, 0:D], xsmp[:, :], ACT.Square, accum_out=small[0:NSEQ, 0:1]))
            act.activation(small[0:NSEQ, 1:2], small[0:NSEQ, 0:1], ACT.Sqrt, bias=eps[0:NSEQ, :],
                           scale=1.0 / D).then_inc(rsm, 1)

            sa, fe, rd = ctr(sqa, fev, rs)

            def normed(m, x, norm, square_to):
                act.activation(a_hi[:, m, :] if isinstance(m, int) else
                               a_hi[:, bass.ds(m, 1), :].rearrange("p a t -> p (a t)"),
                               x, ACT.Copy, scale=vecs[:, m, NORMS[norm]:NORMS[norm] + 1] if isinstance(m, int) else
                               vecs[:, bass.ds(m, 1), NORMS[norm]:NORMS[norm] + 1].rearrange("p a o -> p (a o)"))\
                   .then_inc(ahi, 1)
                squares(x, square_to)

            def squares_free():
                act.wait_ge(sqa, sa.value)

            def squares(x, square_to):
                act.activation(square_to, x, ACT.Square).then_inc(sqr, 1)
                sa.up()

            def roots():
                act.wait_ge(rs, rd.up())
                act.activation(rinv[:, 0:S], PS[:, 6 * BANK:8 * BANK], ACT.Sqrt, bias=eps[:, :], scale=1.0 / D)
                act.activation(rinv[:, S:T], PS[:, RS_TAIL:RS_TAIL + NSEQ], ACT.Sqrt, bias=eps[:, :],
                               scale=1.0 / D).then_inc(rq, 1)

            act.wait_ge(vec_d, 1)
            for m in range(KT):
                if m > 0:
                    squares_free()
                act.wait_ge(fev, fe.up())
                normed(m, xf[m % 2][:, :], "mix0", sqt0[:, :])
                if m == 0:
                    high(0, cols=H, fresh=True)
                    high(1, fresh=True)
            roots()
            high(0)
            act.wait_ge(fz, 1)
            then(act.activation(ge[:, :], gz[:, :], ACT.Abs))
            act.activation(ge[:, :], ge[:, :], ACT.Exp, scale=-1.0).then_inc(fa, 1)
            act.wait_ge(fz, 2)
            act.activation(gd[:, :], gw[:, :], ACT.Ln).then_inc(fa, 1)
            act.wait_ge(ready, 1)
            evc[0].up()

            tk, sdc, ptc, mx, pn, pv, s5, oac, kd, vd, zf = ctr(tkt, sd, ptd, mxd, pnd, pvd, sa5, oad, ktd, vtd, pzd)
            kd.step = vd.step = 16
            ow = Count(osp, 16)
            plc = Count(ptl)
            gran = [1, 2, 3, 4] * 2

            def pair(i, first=False, sample=True):
                high(0)
                act.wait_ge(ev[0], evc[0].up())
                act.activation(q_hi[:, :], qv_raw[:, 0:S], ACT.Copy).then_inc(qkv_h, 1)
                act.wait_ge(ev[1], evc[1].up())
                act.activation(k_hi[:, :], k_raw[:, 0:S], ACT.Copy).then_inc(qkv_h, 1)
                evc[0].up()
                if sample:
                    act.wait_ge(sa5, s5.up())
                    act.activation(ps[:, :, :], z[:, :, :], ACT.Exp).then_inc(sa6, 1)
                if not first:
                    act.wait_ge(ktd, kd.up())
                for n in range(2):
                    act.wait_ge(tkt, tk.up())
                    act.activation(k_tok[:, 4 * n:4 * n + 4, :], bank(4 + n).rearrange("p (t c) -> p t c", c=P),
                                   ACT.Copy).then_inc(tke, 1)
                    then_count()
                act.wait_ge(tke, tkv.value)
                act.dma_start(k_out[:, :, bass.ds(i * P, P)], k_tok[:, :, :]).then_inc(ktd, 16)
                if not first:
                    act.wait_ge(vtd, vd.up())
                for n in range(2):
                    act.wait_ge(tkt, tk.up())
                    act.activation(v_tok[:, 4 * n:4 * n + 4, :], bank(4 + n).rearrange("p (t c) -> p t c", c=P), ACT.Copy)
                    for h in range(2):
                        ins = act.activation(v_pack[:, 4 * n:4 * n + 4, h, 0, :],
                                             bank(4 + n).rearrange("p (t h c) -> p t h c", h=2, c=DH)[:, :, h, :],
                                             ACT.Copy)
                    ins.then_inc(tke, 1)
                    then_count()
                act.wait_ge(tke, tkv.value)
                act.dma_start(v_out[:, :, bass.ds(i * P, P)], v_tok[:, :, :]).then_inc(vtd, 16)
                slot = [0]

                def exponentials(n, t):
                    h, jj = n // 4, n % 4
                    t += 2 * jj
                    k = 8 * h + t
                    w = P * (t + 1)
                    act.wait_ge(mxd, mx.up())
                    if t % 2 == 0:
                        act.wait_ge(pzd, zf.up())
                    act.activation(probs[(n % 2) * 2 + t % 2][:, 0:w],
                                   PS[:, 2 * (t % 2) * BANK:2 * (t % 2) * BANK + w], ACT.Exp,
                                   bias=nmax[:, k:k + 1], accum_out=lsum[:, k:k + 1]).then_inc(exd, 1)

                def high_transposed(g, n):
                    act.wait_ge(ptd, ptc.up())
                    if not (first and n <= 2 and g == 0):
                        act.wait_ge(pvd, pv.up())
                    act.activation(pt_hi[slot[0] % 2][:, :], bank(4 + slot[0] % 2), ACT.Copy).then_inc(pth, 1)
                    slot[0] += 1

                def output_half(n):
                    h, jj = n // 4, n % 4
                    for _ in range(jj + 1):
                        opd.up()
                    act.wait_ge(pvd, opd.value)
                    if not (first and n == 0):
                        act.wait_ge(oad, oac.up())
                    rows = (P - DH, P) if h == 0 else (0, DH)
                    act.activation(o_tmp[h * DH:(h + 1) * DH, :], PS[rows[0]:rows[1], 6 * BANK:6 * BANK + 256],
                                   ACT.Copy).then_inc(ocp, 1)

                for n in range(10):
                    if n < 8:
                        exponentials(n, 0)
                    if n >= 2:
                        output_half(n - 2)
                    groups = (n - 1) % 4 + 1 if 0 < n < 9 else 0
                    for g in range(min(2, groups)):
                        high_transposed(g, n)
                    if n < 8:
                        exponentials(n, 1)
                    if n == 2:
                        high(1)
                    if n == 3:
                        high(0)
                    for g in range(2, groups):
                        high_transposed(g, n)
                act.wait_ge(oad, oac.value + 1)
                act.dma_start(o_spill[bass.ds(i, 1), :, :].rearrange("a p t -> p (a t)"), o_pair[:, :]).then_inc(osp, 16)

            tkv = Count(tke)

            def then_count():
                tkv.up()

            opd = Count(pvd)
            pair(0, first=True, sample=False)
            with counted_loop(act, 1, NPAIR, {wr[0]: 2, wr[1]: 1, done[0]: 2, done[1]: 1, evc[0]: 2, evc[1]: 1, tk: 4, tkv: 4,
                                              mx: 16, ptc: 20, pv: 20, oac: 8, kd: 1, vd: 1, s5: 1, zf: 8,
                                              opd: 20}) as i:
                pair(i)
            act.wait_ge(sa5, s5.up())
            act.activation(ps[:, :, :], z[:, :, :], ACT.Exp).then_inc(sa6, 1)

            oc = Count(oas)
            for m in range(KT):
                act.wait_ge(oas, oc.up())
                act.activation(b_hi[:, m, :], (t0, t1)[m % 2][:, :], ACT.Copy).then_inc(bhi, 1)

            def tile(t, m):
                return t[:, bass.ds(m, 1), :].rearrange("p a t -> p (a t)")

            def out_highs(norm, last=False):
                def turn(i, more=True):
                    for s in range(2):
                        if more:
                            high(s)
                        if norm:
                            squares_free()
                            act.wait_ge(ev[s], evc[s].up())
                            x = tile(x_res, 2 * i + s)
                            if norm == "final":
                                squares(x, t3[:, :])
                            else:
                                normed(2 * i + s, x, norm, t3[:, :])
                        else:
                            evc[s].up()
                per = {wr[0]: 1, wr[1]: 1, done[0]: 1, done[1]: 1, evc[0]: 1, evc[1]: 1}
                if norm:
                    per[sa] = 2
                with counted_loop(act, 0, KT // 2 - (1 if last else 0), per) as i:
                    turn(i)
                if last:
                    turn(KT // 2 - 1, False)
                if norm:
                    roots()

            pr = Count(prd)

            def ffn_highs(norm):
                for c, n in enumerate(CHUNKS):
                    with counted_loop(act, 0, n, {wr[0]: 1, wr[1]: 1, done[0]: 1, done[1]: 1, evc[0]: 1, evc[1]: 1,
                                                  pr: 1}) as j:
                        high(0)
                        act.wait_ge(ev[0], evc[0].up())
                        act.activation(t0[:, :], t0[:, :], ACT.Silu).then_inc(sil, 1)
                        high(1)
                        evc[1].up()
                        act.wait_ge(prd, pr.up())
                        act.activation(tile(b_hi, j), t1[:, :], ACT.Copy).then_inc(bhi, 1)
                    end = c == len(CHUNKS) - 1
                    out_highs(norm if end else None, last=end and norm == "final")

            out_highs("ffn0")
            ffn_highs("mix1")
            with counted_loop(act, 0, KT // 2, {wr[0]: 3, wr[1]: 3, done[0]: 3, done[1]: 3, evc[0]: 3, evc[1]: 3,
                                                pr: 2}) as i:
                for r in range(6):
                    high(r % 2)
                    evc[r % 2].up()
                    if r % 3 == 2:
                        act.wait_ge(prd, pr.up())
                        act.activation(tile(b_hi, 2 * i + r // 3), t3[:, :], ACT.Copy).then_inc(bhi, 1)
            for n in range(2):
                act.wait_ge(cvp, 1)
                act.activation(t0[0:2 + NSEQ, n * BANK:(n + 1) * BANK], PS[0:2 + NSEQ, (6 + n) * BANK:(7 + n) * BANK],
                               ACT.Copy).then_inc(cvc, 1)
            act.wait_ge(cvc, 2)
            act.dma_start(conv_prompt.rearrange("l o j d -> (l o j) d"), t0[0:2, 0:D]).then_inc(outs, 16)
            act.dma_start(conv_sample[0, :, 1, :], t0[2:2 + NSEQ, 0:D]).then_inc(outs, 16)
            act.wait_ge(outs, 32)
            out_highs("ffn1")
            ffn_highs("final")
            yc = Count(ytt)
            for m in range(KT):
                s = m % 2
                act.wait_ge(ytt, yc.up())
                act.activation(y_tok[:, :, m * P:(m + 1) * P],
                               PS[:, 3 * s * BANK:3 * s * BANK + S].rearrange("p (t c) -> p t c", c=P), ACT.Copy)\
                   .then_inc(yte, 1)
                ins = act.activation(y_smp[:, m * P:(m + 1) * P],
                                     PS[0:NSEQ, (3 * s + 2) * BANK:(3 * s + 2) * BANK + P], ACT.Copy)
                ins.then_inc(yte, 1)

        @block.tensor
        def _(pe):
            wlo = [Count(w_lod[s]) for s in range(2)]
            evd = [Count(ev[s]) for s in range(2)]

            def product(s, hi, lo, kts=KT, fresh=False):
                pe.wait_ge(w_lod[s], wlo[s].up())
                if not fresh:
                    pe.wait_ge(ev[s], evd[s].up())
                g = group(s)
                for k in range(kts):
                    for n, (w, x) in enumerate(((w_hi[s], hi), (w_hi[s], lo), (w_lo[s], hi))):
                        for b in range(NB):
                            ins = pe.matmul(g[:, b, :], w[:, k, :], x[:, k, b * TB:(b + 1) * TB],
                                            start=k == 0 and n == 0, stop=k == kts - 1 and n == 2)
                ins.then_inc(mm[s], 1)

            pe.wait_ge(cst, 7)
            pe.wait_ge(vrow_in, 80)
            for k in range(KT):
                ins = pe.transpose(PS[:, 6 * BANK + 24 * k:6 * BANK + 24 * (k + 1)], vrow[:, k * P:(k + 1) * P],
                                   ident[0:24, 0:24])
            ins.then_inc(vec_t, 1)
            pe.wait_ge(x_in, 32)
            for k in range(KT):
                s = k % 2
                if k >= 2:
                    pe.wait_ge(fev, k - 1)
                base = 3 * s * BANK
                for t in range(TT):
                    pe.transpose(PS[:, base + t * P:base + (t + 1) * P], xtok[:, t, k * P:(k + 1) * P], ident[:, :])
                pe.transpose(PS[:, base + S:base + T], xsmp[:, k * P:(k + 1) * P], ident[0:NSEQ, 0:NSEQ])\
                  .then_inc(ftr, 1)

            sq = Count(sqa)

            def sum_squares(total):
                for _ in range(KT):
                    sq.up()
                pe.wait_ge(sqa, sq.value)
                pe.matmul(bank(6), ones[:, :], total[:, 0:BANK], start=True, stop=True)
                pe.matmul(bank(7), ones[:, :], total[:, BANK:S], start=True, stop=True)
                pe.matmul(PS[:, RS_TAIL:RS_TAIL + NSEQ], ones[:, :], total[:, S:T], start=True, stop=True)\
                  .then_inc(rs, 1)

            pe.wait_ge(fev, KT)
            pe.wait_ge(vec_d, 1)
            sum_squares(sqs0)
            lo_parts = Count(alo)

            def normed_ready():
                for _ in range(KT):
                    lo_parts.up()
                pe.wait_ge(alo, lo_parts.value)

            normed_ready()
            product(0, a_hi, a_lo, fresh=True)
            pe.wait_ge(hsd, 1)
            pe.wait_ge(rq, 1)
            for n in range(3 * D // 256):
                pe.wait_ge(wsg[n % 2], 16 * (n // 2 + 1))
                if n >= 2:
                    pe.wait_ge(sme, n - 1)
                for k in range(KT):
                    ins = pe.matmul(PS[0:NSEQ, (6 + n % 2) * BANK:(6 + n % 2) * BANK + 256], hs[:, k, :],
                                    wseg[n % 2][:, k, :], start=k == 0, stop=k == KT - 1)
                ins.then_inc(smm, 1)
            pe.wait_ge(lgt_in, 1)
            pe.wait_ge(sme, 3 * D // 256)
            for t in range(TT):
                pe.transpose(PS[:, 6 * BANK + t * H:6 * BANK + (t + 1) * H], gz[:, t * P:(t + 1) * P], ident[0:H, 0:H])
            pe.transpose(PS[0:NSEQ, 6 * BANK + TT * H:6 * BANK + (TT + 1) * H], gz[:, S:T], ident[0:H, 0:H])\
              .then_inc(lgt, 1)
            pe.wait_ge(lct, 1)
            pe.wait_ge(lgo, 1)
            pe.matmul(bank(7, 0, H), suffix[:, :], tot[:, :], start=True, stop=False)
            pe.matmul(bank(7, 0, H), owner[:, :], lt[0:NSEQ, TT * H:(TT + 1) * H], start=False, stop=True).then_inc(lco, 1)
            pe.wait_ge(lcb, 1)
            for h in range(H):
                if h % 4 == 0 and h >= 8:
                    pe.wait_ge(lbe, h // 4 - 1)
                ins = pe.transpose(PS[:, (6 + h // 4 % 2) * BANK + h % 4 * P:(6 + h // 4 % 2) * BANK + (h % 4 + 1) * P],
                                   lf[:, :].rearrange("p (r h) -> p r h", h=H)[:, :, h], ident[:, :])
                if h % 4 == 3:
                    ins.then_inc(lbt, 1)
            pe.wait_ge(ready, 1)

            s1, s3, s6, s7, s9, ql, tl, te, ex, pn, pl, oa, se = ctr(
                sa1, sa3, sa6, sa7, sa9, qkv_l, tkl, tke, exd, pnd, ptl, oad, seld)
            vi = [Count(vin[n], 16) for n in range(VSLOT)]
            so = Count(so1)

            def sample_max():
                pe.wait_ge(sa1, s1.up())
                pe.transpose(PS[0:H, 7 * BANK + S_MAX:7 * BANK + S_MAX + P], zmax[:, :], ident[:, :]).then_inc(sa2, 1)

            def sample_spread():
                pe.wait_ge(sa3, s3.up())
                pe.matmul(bank(7, S_SPREAD, S_SPREAD + H), ones[0:H, :], mdiag[:, :], start=True, stop=True)\
                  .then_inc(sa4, 1)

            def quadrant(j, a, b):
                return PS[32 * j:32 * j + HQ, 7 * BANK + a:7 * BANK + b]

            def sample_sum():
                pe.wait_ge(sa6, s6.up())
                pe.wait_ge(sa7, s7.up())
                for j in range(4):
                    pe.matmul(quadrant(j, S_SUM, S_SUM + 1), psum_s[:, HQ * j:HQ * (j + 1)], ones[:, 0:1],
                              start=True, stop=True)

            def value_page(g):
                pe.wait_ge(vin[g % VSLOT], vi[g % VSLOT].up())
                for j in range(4):
                    ins = pe.matmul(quadrant(j, S_OUT, S_OUT + 256), ps[:, g, HQ * j:HQ * (j + 1)],
                                    vpage[:, g % VSLOT, 256 * j:256 * (j + 1)], start=g == 0, stop=False)
                ins.then_inc(vfr, 1)

            def value_new():
                for j in range(4):
                    ins = pe.matmul(quadrant(j, S_OUT, S_OUT + 256), ps[0:NSEQ, NPG, HQ * j:HQ * (j + 1)],
                                    v_s[:, 256 * j:256 * (j + 1)], start=False, stop=True)
                ins.then_inc(sa8, 1)

            def sample_turn():
                pe.wait_ge(so1, so.up())
                for c in range(2):
                    ins = pe.transpose(bank(7, S_OUT + c * P, S_OUT + (c + 1) * P), o_rows[:, c * P:(c + 1) * P],
                                       ident[:, :])
                ins.then_inc(so2, 1)

            def rows(h):
                return slice(h * DH, (h + 1) * DH)

            def scores(h, t):
                base = 2 * (t % 2) * BANK
                r = rows(h)
                width = max(256, P * (t + 1))
                spans = [(0, min(BANK, width))] + ([(BANK, max(BANK + 256, width))] if width > BANK else [])
                q = slice(t * P, (t + 1) * P)
                for a, b in spans:
                    out = PS[:, base + a:base + b]
                    diagonal = a <= t * P < b
                    pe.matmul(out, q_hi[r, q], k_hi[r, a:b], start=True, stop=False)
                    pe.matmul(out, q_lo[r, q], k_hi[r, a:b], start=False, stop=False)
                    pe.matmul(out, q_hi[r, q], k_lo[r, a:b], start=False, stop=False)
                    ins = pe.matmul(out, sel[h][r, :], negcum[r, a:b], start=False, stop=not diagonal)
                    if diagonal:
                        ins = pe.matmul(PS[:, base + t * P:base + (t + 1) * P], ident_b[:, :], mask_b[:, :],
                                        start=False, stop=True)
                ins.then_inc(sd, 1)

            def transpose_group(n, g, slot):
                for k in range(2):
                    for t in range(2):
                        ins = pe.transpose(bank(4 + slot % 2, (2 * k + t) * P, (2 * k + t + 1) * P),
                                           probs[(n % 2) * 2 + t][:, (2 * g + k) * P:(2 * g + k + 1) * P], ident[:, :])
                ins.then_inc(ptd, 1)

            def value_group(h, jj, g, slot, new=False):
                pe.wait_ge(ptl, pl.up())
                if g == 0 and not new:
                    pe.wait_ge(oad, oa.up())
                for k in range(2):
                    kt = 2 * g + k
                    v = v_pack[:, kt, h, :, :].rearrange("p a d -> p (a d)")
                    pe.matmul(PS[:, 6 * BANK:6 * BANK + 256], v, pt_hi[slot % 2][:, 256 * k:256 * (k + 1)],
                              start=kt == 0, stop=False)
                    ins = pe.matmul(PS[:, 6 * BANK:6 * BANK + 256], v, pt_lo[slot % 2][:, 256 * k:256 * (k + 1)],
                                    start=False, stop=kt == 2 * jj + 1)
                ins.then_inc(pvd, 1)

            def pair(first, sample=True):
                if not first:
                    pe.wait_ge(exd, ex.value)
                    pe.wait_ge(ptl, pl.value)
                product(0, a_hi, a_lo)
                if sample:
                    sample_max()
                product(1, a_hi, a_lo, fresh=first)
                product(0, a_hi, a_lo)
                if sample:
                    sample_spread()
                pe.wait_ge(ev[1], evd[1].value + 1)
                for n in range(2):
                    for t in range(4):
                        ins = pe.transpose(bank(4 + n, t * P, (t + 1) * P), k_raw[:, (4 * n + t) * P:(4 * n + t + 1) * P],
                                           ident[:, :])
                    ins.then_inc(tkt, 1)
                pe.wait_ge(ev[0], evd[0].value + 1)
                for n in range(2):
                    pe.wait_ge(tke, te.up())
                    for t in range(4):
                        ins = pe.transpose(bank(4 + n, t * P, (t + 1) * P), qv_raw[:, (4 * n + t) * P:(4 * n + t + 1) * P],
                                           ident[:, :])
                    ins.then_inc(tkt, 1)
                te.up()
                te.up()
                if sample:
                    sample_sum()
                pe.wait_ge(qkv_l, ql.up())
                pe.wait_ge(qkv_l, ql.up())
                pe.wait_ge(seld, se.up())
                slot = 0
                for n in range(9):
                    def score(t, n=n):
                        if n > 0:
                            pe.wait_ge(exd, ex.up())
                        scores(n // 4, 2 * (n % 4) + t)

                    if n < 8:
                        score(0)
                        if sample:
                            value_page(2 * n)
                    elif sample:
                        value_new()
                    if n > 0:
                        h, jj = (n - 1) // 4, (n - 1) % 4
                        if n == 1:
                            tl.up()
                            pe.wait_ge(tkl, tl.up())
                        pn.up()
                        pe.wait_ge(pnd, pn.up())
                        for g in range(min(2, jj + 1)):
                            transpose_group(n - 1, g, slot + g)
                    if n < 8:
                        score(1)
                    if n > 0:
                        for g in range(jj + 1):
                            value_group(h, jj, g, slot + g, first and n == 1)
                            if g + 2 <= jj:
                                transpose_group(n - 1, g + 2, slot + g + 2)
                            if g == 0 and n < 8 and sample:
                                value_page(2 * n + 1)
                        slot += jj + 1
                    elif sample:
                        value_page(1)
                if sample:
                    sample_turn()
                ex.up()
                ex.up()

            pair(True, sample=False)
            with counted_loop(pe, 1, NPAIR, {s1: 1, s3: 1, s6: 1, s7: 1, so: 1, ql: 2, tl: 2, te: 4, ex: 16, pn: 16,
                                             pl: 20, oa: 8, se: 1, wlo[0]: 2, wlo[1]: 1, evd[0]: 2, evd[1]: 1,
                                             **{vi[n]: 8 for n in range(VSLOT)}}) as i:
                pair(False)
            sample_max()
            sample_spread()
            sample_sum()
            for g in range(NPG):
                value_page(g)
            value_new()
            sample_turn()

            bl = Count(blo)

            def out_product(kts):
                with counted_loop(pe, 0, KT // 2, {wlo[0]: 1, wlo[1]: 1, evd[0]: 1, evd[1]: 1}) as i:
                    product(0, b_hi, b_lo, kts)
                    product(1, b_hi, b_lo, kts)

            def parts_ready(n):
                for _ in range(n):
                    bl.up()
                pe.wait_ge(blo, bl.value)

            def next_norm():
                pe.wait_ge(ev[0], evd[0].value + 1)
                pe.wait_ge(ev[1], evd[1].value + 1)
                sum_squares(t2)

            rqc = Count(rq)
            rqc.up()

            def ffn():
                pe.wait_ge(rq, rqc.up())
                normed_ready()
                for n in CHUNKS:
                    with counted_loop(pe, 0, n, {wlo[0]: 1, wlo[1]: 1, evd[0]: 1, evd[1]: 1}) as j:
                        product(0, a_hi, a_lo)
                        product(1, a_hi, a_lo)
                    parts_ready(n)
                    out_product(n)
                next_norm()

            parts_ready(KT)
            pe.wait_ge(sa9, NSEQ)
            out_product(KT)
            next_norm()
            ffn()
            pe.wait_ge(rq, rqc.up())
            normed_ready()
            with counted_loop(pe, 0, KT // 2, {wlo[0]: 3, wlo[1]: 3, evd[0]: 3, evd[1]: 3}) as i:
                for r in range(6):
                    product(r % 2, a_hi, a_lo)
            pe.wait_ge(cvt, KT)
            for m in range(KT):
                ins = pe.transpose(PS[0:2 + NSEQ, 6 * BANK + m * P:6 * BANK + (m + 1) * P], conv_rows[:, m, :], ident[:, :])
            ins.then_inc(cvp, 1)
            parts_ready(KT)
            out_product(KT)
            pe.wait_ge(cvc, 2)
            next_norm()
            ffn()
            yc, ye = ctr(yt, yte)
            for m in range(KT):
                s = m % 2
                pe.wait_ge(yt, yc.up())
                if m >= 2:
                    pe.wait_ge(yte, 2 * (m - 1))
                base = 3 * s * BANK
                for t in range(TT):
                    pe.transpose(PS[:, base + t * P:base + (t + 1) * P], x_res[:, m, t * P:(t + 1) * P], ident[:, :])
                pe.transpose(PS[0:NSEQ, base + 2 * BANK:base + 2 * BANK + P], x_res[:, m, S:T], ident[:, :])\
                  .then_inc(ytt, 1)

        @block.vector
        def _(dve):
            steps = Count(dv)

            def then(ins):
                ins.then_inc(dv, 1)
                dve.wait_ge(dv, steps.up())

            done = [Count(mm[s]) for s in range(2)]
            ah, rqc, rrc = ctr(ahi, rq, rr)

            def low_normed(m, x, norm):
                dve.wait_ge(ahi, ah.up())
                if isinstance(m, int):
                    out, hi, g = a_lo[:, m, :], a_hi[:, m, :], vecs[:, m, NORMS[norm]:NORMS[norm] + 1]
                else:
                    out = a_lo[:, bass.ds(m, 1), :].rearrange("p a t -> p (a t)")
                    hi = a_hi[:, bass.ds(m, 1), :].rearrange("p a t -> p (a t)")
                    g = vecs[:, bass.ds(m, 1), NORMS[norm]:NORMS[norm] + 1].rearrange("p a o -> p (a o)")
                dve.scalar_tensor_tensor(out=out, in0=x, scalar=g, in1=hi.bitcast(F32), op0=ALU.mult,
                                         op1=ALU.subtract).then_inc(alo, 1)

            def reciprocals():
                dve.wait_ge(rq, rqc.up())
                dve.reciprocal(rinv[:, :], rinv[:, :]).then_inc(rr, 1)
                dve.wait_ge(rr, rrc.up())

            def read_out(s, out, scale=1.0):
                dve.wait_ge(mm[s], done[s].up())
                return dve.scalar_tensor_tensor(out=blocks(out), in0=group(s), scalar=scale, in1=blocks(rinv[:, :]),
                                                op0=ALU.mult, op1=ALU.mult)

            dve.wait_ge(vec_t, 1)
            dve.wait_ge(cst, 7)
            dve.tensor_copy(vecs[:, :, :].rearrange("p k r -> p (k r)"), PS[:, 6 * BANK:6 * BANK + 24 * KT])\
               .then_inc(vec_d, 1)
            dve.tensor_copy(ident_b[:, :], ident[:, :])
            dve.tensor_copy(mask_b[:, :], mask_f[:, :])
            dve.wait_ge(rsm, 1)
            dve.reciprocal(small[0:NSEQ, 2:3], small[0:NSEQ, 1:2])
            dve.wait_ge(vec_d, 1)
            alc = Count(alo)
            for m in range(KT):
                s = m % 2
                dve.wait_ge(ftr, m + 1)
                if m >= 2:
                    dve.wait_ge(xsp[s], 16 * (m // 2))
                    dve.wait_ge(sqr, m - 1)
                    dve.wait_ge(alo, m - 1)
                dve.tensor_copy(xf[s][:, :], PS[:, 3 * s * BANK:3 * s * BANK + T]).then_inc(fev, 1)
                dve.wait_ge(fev, m + 1)
                low_normed(m, xf[s][:, :], "mix0")
            dve.wait_ge(alo, KT)
            dve.tensor_tensor(hs[:, :, :], a_hi[:, :, S:T].bitcast(F32), a_lo[:, :, S:T].bitcast(F32), ALU.add)\
               .then_inc(hsd, 1)
            reciprocals()
            dve.wait_ge(mm[0], done[0].up())
            dve.scalar_tensor_tensor(out=blocks(gz[:, :]), in0=group(0)[0:H], scalar=1.0, in1=blocks(rinv[0:H, :]),
                                     op0=ALU.mult, op1=ALU.mult).then_inc(ev[0], 1)
            dve.wait_ge(ev[0], 1)
            dve.wait_ge(misc_in, 48)
            dve.tensor_scalar(gz[:, :], gz[:, :], bf_col[:, 0:1], None, ALU.add).then_inc(fz, 1)
            dve.wait_ge(fa, 1)
            dve.tensor_scalar(gw[:, :], ge[:, :], 1.0, None, ALU.add).then_inc(fz, 1)
            for n in range(3 * D // 256):
                dve.wait_ge(smm, n + 1)
                dst = (q_s, k_s, v_s)[n // 4]
                dve.tensor_scalar(dst[:, n % 4 * 256:(n % 4 + 1) * 256],
                                  PS[0:NSEQ, (6 + n % 2) * BANK:(6 + n % 2) * BANK + 256], small[0:NSEQ, 2:3],
                                  QS if n < 4 else 1.0, ALU.mult, ALU.mult).then_inc(sme, 1)
            dve.wait_ge(fa, 2)
            gln = gd
            dve.wait_ge(sqa, KT)
            then(dve.tensor_scalar(gw[:, :], gw[:, :], 1.0, None, ALU.subtract))
            then(dve.tensor_scalar(sqt0[0:H, :], gw[:, :], 0.0, None, ALU.is_equal))
            then(dve.tensor_tensor(gw[:, :], gw[:, :], sqt0[0:H, :], ALU.add))
            then(dve.reciprocal(gw[:, :], gw[:, :]))
            then(dve.tensor_tensor(gw[:, :], gw[:, :], ge[:, :], ALU.mult))
            then(dve.tensor_tensor(gw[:, :], gw[:, :], gln[:, :], ALU.mult))
            then(dve.tensor_tensor(ge[:, :], ge[:, :], sqt0[0:H, :], ALU.mult))
            then(dve.tensor_tensor(gw[:, :], gw[:, :], ge[:, :], ALU.add))
            dve.scalar_tensor_tensor(out=gz[:, :], in0=gz[:, :], scalar=0.0, in1=gw[:, :], op0=ALU.min,
                                     op1=ALU.subtract).then_inc(lgt_in, 1)
            dve.wait_ge(lgt_in, 1)
            dve.wait_ge(lgt, 1)
            dve.tensor_copy(lt[:, 0:TT * H], PS[:, 6 * BANK:6 * BANK + TT * H])
            dve.tensor_copy(lt[0:NSEQ, TT * H:(TT + 1) * H], PS[0:NSEQ, 6 * BANK + TT * H:6 * BANK + (TT + 1) * H])\
               .then_inc(lgo, 1)
            then(dve.memset(sqt0[0:H, :], 1.0))
            then(dve.tensor_tensor_scan(ge[:, 0:S], sqt0[0:H, 0:S], gz[:, 0:S], 0.0, ALU.mult, ALU.add))
            then(dve.tensor_scalar(ge[:, 0:S], ge[:, 0:S], -1.0, None, ALU.mult))
            then(dve.tensor_copy(negcum[0:H, :], ge[:, 0:S]))
            then(dve.tensor_tensor(negcum[32:32 + H, :], ge[:, 0:S], negcum[0:H, :].bitcast(F32), ALU.subtract))
            then(dve.tensor_copy(negcum[64:64 + H, :], negcum[0:H, :].bitcast(F32)))
            then(dve.tensor_copy(negcum[96:96 + H, :], negcum[32:32 + H, :].bitcast(F32)))
            then(dve.tensor_tensor(sqs0[0:NSEQ, 0:D], q_s[:, :], k_s[:, :], ALU.mult))
            then(dve.tensor_reduce(snew_row[:, :], sqs0[0:NSEQ, 0:D].rearrange("p (h d) -> p h d", d=DH), X_AXIS, ALU.add))
            then(dve.tensor_scalar(negd[:, :], ident[0:NSEQ, 0:NSEQ], -1.0, -NEG_INF, ALU.add, ALU.mult))
            rows_h = snew_row[:, :].unsqueeze(1).to_broadcast([NSEQ, NSEQ, H])
            cols_b = ident[0:NSEQ, 0:NSEQ].unsqueeze(2).to_broadcast([NSEQ, NSEQ, H])
            neg_b = negd[:, :].unsqueeze(2).to_broadcast([NSEQ, NSEQ, H])
            then(dve.tensor_tensor(s_new[0:NSEQ, :, :], rows_h, cols_b, ALU.mult))
            then(dve.tensor_tensor(s_new[0:NSEQ, :, :], s_new[0:NSEQ, :, :], neg_b, ALU.add))
            dve.wait_ge(lf_in, 16)
            then(dve.memset(sqt0[:, 0:PAGE], 1.0))
            lf3 = lf[:, :].rearrange("p (r h) -> p h r", h=H)
            lc3 = lc[:, :].rearrange("p (r h) -> p h r", h=H)
            for h in range(H):
                ins = dve.tensor_tensor_scan(lc3[:, h, :], sqt0[:, 0:PAGE], lf3[:, h, :], 0.0, ALU.mult, ALU.add)
            then(ins)
            dve.tensor_copy(tot[:, :], lc[:, (PAGE - 1) * H:PAGE * H]).then_inc(lct, 1)
            dve.wait_ge(lco, 1)
            dve.wait_ge(lct, 1)
            then(dve.tensor_copy(tot[:, :], bank(7, 0, H)))
            dve.tensor_tensor(lf[:, :].rearrange("p (r h) -> p r h", h=H),
                              tot[:, :].unsqueeze(1).to_broadcast([P, PAGE, H]),
                              lc[:, :].rearrange("p (r h) -> p r h", h=H), ALU.subtract).then_inc(lcb, 1)
            for n in range(4):
                dve.wait_ge(lbt, n + 1)
                dve.tensor_copy(s_bias[:, 4 * n:4 * n + 4, :].rearrange("p h g -> p (h g)"), bank(6 + n % 2))\
                   .then_inc(lbe, 1)
            dve.wait_ge(lbe, 4)
            dve.wait_ge(w_lod[0], 1)
            dve.wait_ge(sqa, KT)
            dve.wait_ge(out0, 64)
            dve.wait_ge(qsp, 16)
            dve.nop().then_inc(ready, 1)

            qh, ex, pt, oc, kf, km, s2, s4, s6, s8, s9, te = ctr(
                qkv_h, exd, pth, ocp, kfr, kml, sa2, sa4, sa6, sa8, so2, tke)
            dve.memset(bank(7), 1.0)
            kp = [Count(kin[n], 16) for n in range(KSLOT)]
            qb = Count(qbi, 16)
            ow = Count(osp, 16)
            sdc, pvc = ctr(sd, pvd)
            plc, pnc, mxc = ctr(ptl, pnd, mxd)

            def key_page(g, first):
                slot = kpage[:, g % KSLOT, :]
                dve.wait_ge(kin[g % KSLOT], kp[g % KSLOT].up())
                if g == 0:
                    dve.wait_ge(qbi, qb.up())
                if g in POOL_K:
                    dve.wait_ge(kml, km.up())
                else:
                    then(dve.tensor_tensor(slot, slot, q_bc[:, :], ALU.mult))
                dve.tensor_reduce(s_raw[:, g, :], slot.rearrange("p (h d) -> p h d", d=DH), X_AXIS, ALU.add)\
                   .then_inc(kfr, 1)
                kf.up()

            def sample_scores(b):
                dve.wait_ge(kfr, kf.value)
                bias = s_bias[:, :, bass.ds(b * NPG, NPG)].rearrange("p h g -> p g h")
                dve.tensor_tensor(z[:, 0:NPG, :], s_raw[:, :, :], bias, ALU.add)
                new = s_new[:, bass.ds(b, 1), :]
                then(dve.tensor_copy(z[:, NPG:NPG + 1, :], new))
                dve.tensor_reduce(zmax[:, :], z[:, :, :].rearrange("p g h -> p h g"), X_AXIS, ALU.max).then_inc(sa1, 1)

            def sample_maxima():
                dve.wait_ge(sa2, s2.up())
                then(dve.tensor_reduce(mcol[:, :], PS[0:H, 7 * BANK + S_MAX:7 * BANK + S_MAX + P], X_AXIS, ALU.max))
                dve.tensor_scalar(mdiag[:, :], ident[0:H, 0:H], mcol[:, 0:1], None, ALU.mult).then_inc(sa3, 1)

            def sample_shift():
                dve.wait_ge(sa4, s4.up())
                dve.tensor_tensor(z[:, :, :], z[:, :, :], bank(7, S_SPREAD, S_SPREAD + H).unsqueeze(1).to_broadcast([P, NPG + 1, H]),
                                  ALU.subtract).then_inc(sa5, 1)

            def sample_sums():
                dve.wait_ge(sa6, s6.up())
                dve.tensor_reduce(psum_s[:, :], ps[:, :, :].rearrange("p g h -> p h g"), X_AXIS, ALU.add).then_inc(sa7, 1)

            def sample_scale():
                dve.wait_ge(sa8, s8.up())
                then(dve.reciprocal(rl[:, :], bank(7, S_SUM, S_SUM + 1)))
                dve.tensor_scalar(o_rows[:, :], bank(7, S_OUT, S_OUT + 256), rl[:, 0:1], None, ALU.mult).then_inc(so1, 1)

            def sample_output(b):
                dve.wait_ge(so2, s9.up())
                for c in range(2):
                    for e in range(2):
                        r = slice(e * DH, (e + 1) * DH)
                        src = bank(7, S_OUT + c * P, S_OUT + (c + 1) * P).rearrange("p (j n) -> p j n", n=32)
                        dst = o_smp[:, :, bass.ds(b, 1)].rearrange("p (j c) b -> p j (c b)", c=2)
                        ins = dve.tensor_copy(dst[r, :, c:c + 1], src[r, :, 2 * c + e:2 * c + e + 1])
                ins.then_inc(sa9, 1)

            def pair(i, first=False, sample=True):
                if sample:
                    sample_scores(i - 1)
                dve.wait_ge(qkv_l, qlc.value) if not first else None
                read_out(0, qv_raw[:, :], QS).then_inc(ev[0], 1)
                evc[0].up()
                dve.wait_ge(ev[0], evc[0].value)
                dve.wait_ge(qkv_h, qh.up())
                dve.tensor_tensor(q_lo[:, :], qv_raw[:, 0:S], q_hi[:, :].bitcast(F32), ALU.subtract).then_inc(qkv_l, 1)
                qlc.up()
                for h in range(2):
                    r = slice(h * DH, (h + 1) * DH)
                    ins = dve.tensor_scalar(sel[h][r, :], ones[r, :], sel_col(i, h)[r, :], None, ALU.mult)
                ins.then_inc(seld, 1)
                for g in range(4):
                    key_page(g, first)
                if sample:
                    sample_maxima()
                read_out(1, k_raw[:, :]).then_inc(ev[1], 1)
                evc[1].up()
                dve.wait_ge(ev[1], evc[1].value)
                dve.wait_ge(qkv_h, qh.up())
                dve.tensor_tensor(k_lo[:, :], k_raw[:, 0:S], k_hi[:, :].bitcast(F32), ALU.subtract).then_inc(qkv_l, 1)
                qlc.up()
                for g in range(4, 8):
                    key_page(g, first)
                dve.wait_ge(qkv_l, qlc.value)
                read_out(0, qv_raw[:, :]).then_inc(ev[0], 1)
                evc[0].up()
                if sample:
                    sample_shift()
                for g in range(8, KEYS_IN_PROJECTION):
                    key_page(g, first)
                if sample:
                    sample_sums()
                te.up()
                te.up()
                for n in range(2):
                    dve.wait_ge(tke, te.up())
                    for h in range(2):
                        ins = dve.tensor_tensor(
                            v_pack[:, 4 * n:4 * n + 4, h, 1, :],
                            bank(4 + n).rearrange("p (t h c) -> p t h c", h=2, c=DH)[:, :, h, :],
                            v_pack[:, 4 * n:4 * n + 4, h, 0, :].bitcast(F32), ALU.subtract)
                    ins.then_inc(tkl, 1)
                slot = [0]

                def maxima(n, t):
                    h, jj = n // 4, n % 4
                    t += 2 * jj
                    dve.wait_ge(sd, sdc.up())
                    base = 2 * (t % 2) * BANK
                    dve.tensor_reduce(nmax[:, 8 * h + t:8 * h + t + 1], PS[:, base:base + P * (t + 1)], X_AXIS,
                                      ALU.max, negate=True).then_inc(mxd, 1)

                def low_transposed(g, n):
                    dve.wait_ge(pth, pt.up())
                    if not (first and n <= 2 and g == 0):
                        dve.wait_ge(pvd, pvc.up())
                    dve.tensor_tensor(pt_lo[slot[0] % 2][:, :], bank(4 + slot[0] % 2),
                                      pt_hi[slot[0] % 2][:, :].bitcast(F32), ALU.subtract).then_inc(ptl, 1)
                    slot[0] += 1

                def output_sum(n):
                    h, jj = n // 4, n % 4
                    dve.wait_ge(ocp, oc.up())
                    if n == 0 and not first:
                        dve.wait_ge(osp, ow.up())
                    r = slice(h * DH, (h + 1) * DH)
                    dve.tensor_tensor(o_pair[r, 256 * jj:256 * (jj + 1)], PS[r, 6 * BANK:6 * BANK + 256],
                                      o_tmp[r, :], ALU.add).then_inc(oad, 1)

                def normalised(n, t):
                    h, jj = n // 4, n % 4
                    t += 2 * jj
                    k = 8 * h + t
                    dve.wait_ge(exd, ex.up())
                    then(dve.reciprocal(lsum[:, k:k + 1], lsum[:, k:k + 1]))
                    pr = probs[(n % 2) * 2 + t % 2][:, 0:P * (t + 1)]
                    dve.tensor_scalar(pr, pr, lsum[:, k:k + 1], None, ALU.mult).then_inc(pnd, 1)

                for n in range(10):
                    if n < 8:
                        maxima(n, 0)
                    if n >= 2:
                        output_sum(n - 2)
                    groups = (n - 1) % 4 + 1 if 0 < n < 9 else 0
                    for g in range(min(2, groups)):
                        low_transposed(g, n)
                    if n < 8:
                        normalised(n, 0)
                        maxima(n, 1)
                    elif n == 8 and sample:
                        sample_scale()
                    for g in range(2, groups):
                        low_transposed(g, n)
                    if n < 8:
                        normalised(n, 1)
                        if n % 2 == 1:
                            key_page(KEYS_IN_PROJECTION + n // 2, first)
                if sample:
                    sample_output(i - 1)

            def sel_col(i, h):
                return sel_id[:, bass.ds(2 * i + h, 1)]

            qlc = Count(qkv_l)
            evc = [Count(ev[s]) for s in range(2)]
            evc[0].value = 1
            pair(0, first=True, sample=False)
            with counted_loop(dve, 1, NPAIR, {
                    qh: 2, ex: 16, pt: 20, oc: 8, kf: 16, km: len(POOL_K), s2: 1, s4: 1, s6: 1, s8: 1, s9: 1, te: 4, qb: 1,
                    ow: 1, sdc: 16, pvc: 20, qlc: 2, evc[0]: 2, evc[1]: 1, done[0]: 2, done[1]: 1,
                    steps: NPG - len(POOL_K) + 16 + 3, **{kp[n]: 4 for n in range(KSLOT)}}) as i:
                pair(i)
            sample_scores(NSEQ - 1)
            sample_maxima()
            sample_shift()
            sample_sums()
            sample_scale()
            sample_output(NSEQ - 1)

            bh = Count(bhi)
            dve.wait_ge(sa9, NSEQ)
            for m in range(KT):
                t = (t0, t1)[m % 2]
                if m >= 2:
                    dve.wait_ge(blo, m - 1)
                dve.wait_ge(oin[m % 2], 16 * (m // 2 + 1))
                dve.tensor_copy(t[:, S:T], o_smp[:, m, :]).then_inc(oas, 1)
                dve.wait_ge(oas, m + 1)
                dve.wait_ge(bhi, bh.up())
                dve.tensor_tensor(b_lo[:, m, :], t[:, :], b_hi[:, m, :].bitcast(F32), ALU.subtract).then_inc(blo, 1)
            dve.wait_ge(blo, KT)
            dve.wait_ge(xin, 16)
            bl = Count(blo)
            bl.value = KT

            def tile(t, m):
                return t[:, bass.ds(m, 1), :].rearrange("p a t -> p (a t)")

            def out_adds(norm=None):
                per = {done[0]: 1, done[1]: 1, evc[0]: 1, evc[1]: 1}
                if norm and norm != "final":
                    per[ah] = 2
                with counted_loop(dve, 0, KT // 2, per) as i:
                    for s in range(2):
                        x = tile(x_res, 2 * i + s)
                        dve.wait_ge(mm[s], done[s].up())
                        dve.tensor_tensor(blocks(x), group(s), blocks(x), ALU.add).then_inc(ev[s], 1)
                        dve.wait_ge(ev[s], evc[s].up())
                        if norm and norm != "final":
                            low_normed(2 * i + s, x, norm)
                if norm:
                    reciprocals()

            sl = Count(sil)
            prc = Count(prd)

            def ffn(norm):
                for c, n in enumerate(CHUNKS):
                    with counted_loop(dve, 0, n, {done[0]: 1, done[1]: 1, evc[0]: 1, evc[1]: 1, sl: 1, prc: 1,
                                                  bl: 1}) as j:
                        dve.wait_ge(blo, bl.value)
                        read_out(0, t0[:, :]).then_inc(ev[0], 1)
                        evc[0].up()
                        read_out(1, t1[:, :]).then_inc(ev[1], 1)
                        dve.wait_ge(ev[1], evc[1].up())
                        dve.wait_ge(sil, sl.up())
                        dve.tensor_tensor(t1[:, :], t1[:, :], t0[:, :], ALU.mult).then_inc(prd, 1)
                        prc.up()
                        bl.up()
                    out_adds(norm if c == len(CHUNKS) - 1 else None)

            out_adds("ffn0")
            ffn("mix1")

            then(dve.memset(t2[:, 0:2], 0.0))
            bh.value = bh.value + HID
            with counted_loop(dve, 0, KT // 2, {done[0]: 3, done[1]: 3, evc[0]: 3, evc[1]: 3, prc: 2, bh: 2, bl: 2,
                                                steps: 2 * 6}) as i:
                for m in range(2):
                    f = 2 * i + m

                    def vec(a, b=None, f=f):
                        return vecs[:, bass.ds(f, 1), a:b or a + 1].rearrange("p a o -> p (a o)")

                    dve.wait_ge(blo, bl.value)
                    read_out(m, t0[:, :]).then_inc(ev[m], 1)
                    evc[m].up()
                    read_out(1 - m, t1[:, :]).then_inc(ev[1 - m], 1)
                    evc[1 - m].up()
                    read_out(m, t2[:, 2:T + 2]).then_inc(ev[m], 1)
                    dve.wait_ge(ev[m], evc[m].up())
                    dve.wait_ge(ev[1 - m], evc[1 - m].value)
                    then(dve.tensor_tensor(t2[:, 2:T + 2], t2[:, 2:T + 2], t1[:, :], ALU.mult))
                    dve.tensor_copy(conv_rows[:, bass.ds(f, 1), :].rearrange("p a r -> p (a r)"), t2[:, S:T + 2])\
                       .then_inc(cvt, 1)
                    then(dve.tensor_scalar(t3[:, :], t2[:, 2:T + 2], vec(TAP + 2), None, ALU.mult))
                    then(dve.scalar_tensor_tensor(out=t3[:, 0:S], in0=t2[:, 1:S + 1], scalar=vec(TAP + 1),
                                                  in1=t3[:, 0:S], op0=ALU.mult, op1=ALU.add))
                    then(dve.scalar_tensor_tensor(out=t3[:, 0:S], in0=t2[:, 0:S], scalar=vec(TAP),
                                                  in1=t3[:, 0:S], op0=ALU.mult, op1=ALU.add))
                    for j in (1, 0):
                        prev = vec(PREV, 24).rearrange("p (b j) -> p b j", j=2)[:, :, j]
                        then(dve.scalar_tensor_tensor(out=t3[:, S:T], in0=prev, scalar=vec(TAP + j),
                                                      in1=t3[:, S:T], op0=ALU.mult, op1=ALU.add))
                    dve.tensor_tensor(t3[:, :], t3[:, :], t0[:, :], ALU.mult).then_inc(prd, 1)
                    dve.wait_ge(prd, prc.up())
                    dve.wait_ge(bhi, bh.up())
                    dve.tensor_tensor(tile(b_lo, f), t3[:, :], tile(b_hi, f).bitcast(F32), ALU.subtract).then_inc(blo, 1)
                    bl.up()
            out_adds("ffn1")
            ffn("final")
            for m in range(KT):
                dve.scalar_tensor_tensor(out=x_res[:, m, :], in0=x_res[:, m, :],
                                         scalar=vecs[:, m, NORMS["final"]:NORMS["final"] + 1], in1=rinv[:, :],
                                         op0=ALU.mult, op1=ALU.mult).then_inc(yt, 1)


_INS = ["x_prompt", "x_sample", "cache_k", "cache_v", "cache_logf", "state_conv", "page_table",
        "norm_mix", "norm_ffn", "w_ffn_in", "w_ffn_out", "norm_final",
        "attn_w_qkvf", "attn_b_f", "attn_w_o", "conv_w_in", "conv_kernel", "conv_w_out"]


def kernel(**inputs):
    import numpy as _np
    import concourse.bacc as _bacc
    from concourse.bass_utils import run_bass_kernel_spmd as _run

    nc = _bacc.Bacc("TRN2", target_bir_lowering=False, num_devices=1, dynamic_dma_scratch_size=4096)
    arrays, args = {}, []
    for name in _INS:
        a = _np.ascontiguousarray(inputs[name])
        arrays[f"in_{name}"] = a
        args.append(nc.dram_tensor(f"in_{name}", a.shape, mybir.dt.from_np(a.dtype), kind="ExternalInput").ap())
    b, s, d = inputs["x_prompt"].shape
    db, ds, _ = inputs["x_sample"].shape
    la, _, _, h, dh = inputs["cache_k"].shape
    lc, _, w1, _ = inputs["state_conv"].shape
    outs = [(b, s, d), (db, ds, d), (la, b, s, h, dh), (la, b, s, h, dh), (la, b, s, h),
            (la, db, ds, h, dh), (la, db, ds, h, dh), (la, db, ds, h), (lc, b, w1, d), (lc, db, w1, d)]
    for i, shape in enumerate(outs):
        args.append(nc.dram_tensor(f"out_{i}", shape, F32, kind="ExternalOutput").ap())
    fox_shortconv_hybrid_step(nc, *args)
    r = _run(nc, [arrays], core_ids=[0])
    return tuple(r.results[0][f"out_{i}"] for i in range(len(outs)))
```

```python
from contextlib import ExitStack, contextmanager

import concourse.bass as bass
from concourse import mybir

F32 = mybir.dt.float32
F32R = mybir.dt.float32r
BF16 = mybir.dt.bfloat16
I32 = mybir.dt.int32
ALU = mybir.AluOpType
ACT = mybir.ActivationFunctionType
X_AXIS = mybir.AxisListType.X

P = 128
NEG_INF = -1e30
RMS_EPS = 1e-6


class Count:

    def __init__(self, semaphore, step=1):
        self.sem, self.step, self.value, self.ups = semaphore, step, 0, 0

    def up(self):
        self.value = self.value + self.step
        self.ups += 1
        return self.value


@contextmanager
def counted_loop(engine, start, end, per):
    bases = {c: (c.value, c.ups) for c in per}
    with engine.Fori(start, end) as i:
        for c, n in per.items():
            c.value = (i - start) * (n * c.step) + c.value if start else i * (n * c.step) + c.value
        yield i
    for c, n in per.items():
        value, ups = bases[c]
        assert c.ups - ups == n, (c.sem, c.ups - ups, n)
        c.value = value + (end - start) * n * c.step


def fox_shortconv_hybrid_step(
    nc, x_prompt, x_sample, cache_k, cache_v, cache_logf, state_conv, page_table,
    norm_mix, norm_ffn, w_ffn_in, w_ffn_out, norm_final,
    attn_w_qkvf, attn_b_f, attn_w_o, conv_w_in, conv_kernel, conv_w_out,
    y_prompt, y_sample, k_prompt, v_prompt, logf_prompt,
    k_sample, v_sample, logf_sample, conv_prompt, conv_sample,
):
    _, S, D = x_prompt.shape
    NSEQ = x_sample.shape[0]
    _, POOL, PAGE, H, DH = cache_k.shape
    NPG = page_table.shape[1]
    DFF = w_ffn_out.shape[1]
    T = S + NSEQ
    KT = D // P
    TT = S // P
    NB = 3
    TB = T // NB
    BANK = 512
    NPAIR = H // 2
    QS = DH ** -0.5
    NPAGES = NSEQ * NPG
    KSLOT, VSLOT = 4, 2
    HID = DFF // P
    CHUNKS = [6, 6, 5, 5]
    assert TB * NB == T and TB <= BANK and PAGE == P and NPAIR == NSEQ == KT == TT == 8
    assert DH * 2 == P and NPG == 16 and NPAGES == P and sum(CHUNKS) == HID

    x_tok = x_prompt.rearrange("o (t p) d -> p (o t) d", p=P)
    x_smp = x_sample.rearrange("b o d -> (b o) d")
    k_pages = cache_k.rearrange("l g p h d -> (l g) p (h d)")
    v_pages = cache_v.rearrange("l g p h d -> (l g) p (h d)")
    logf_pages = cache_logf.rearrange("l g p h -> (l g) (p h)")
    w_qkvf = attn_w_qkvf.rearrange("l k n -> (l k) n")
    w_o = attn_w_o.rearrange("l k n -> (l k) n")
    w_cin = conv_w_in.rearrange("l k n -> (l k) n")
    w_cout = conv_w_out.rearrange("l k n -> (l k) n")
    w_in = [w_ffn_in[l, :, :] for l in range(2)]
    w_out = [w_ffn_out[l, :, :] for l in range(2)]
    k_out = k_prompt.rearrange("l o (t p) h d -> p (l o t) (h d)", p=P)
    v_out = v_prompt.rearrange("l o (t p) h d -> p (l o t) (h d)", p=P)
    x_spill = nc.dram_tensor("x_spill", [KT, P, T], F32, kind="Internal").ap()
    o_spill = nc.dram_tensor("o_spill", [KT, P, S], F32, kind="Internal").ap()
    q_spill = nc.dram_tensor("q_spill", [NSEQ, D], F32, kind="Internal").ap()

    def w_tile(w, row, kts, col):
        return w[row:row + kts * P, bass.ds(col, P)].rearrange("(k p) c -> p k c", p=P)

    ctx = ExitStack()
    with ctx:
        def sb(name, shape, dt, stack=ctx):
            return stack.enter_context(nc.sbuf_tensor(name, shape, dt))

        def sem(name):
            return ctx.enter_context(nc.semaphore(name))

        PS = ctx.enter_context(nc.psum_tensor("PS", [P, 8 * BANK], F32))

        def group(s):
            return PS[:, 3 * s * BANK:3 * (s + 1) * BANK].rearrange("p (b n) -> p b n", b=NB)[:, :, 0:TB]

        def bank(n, a=0, b=BANK):
            return PS[:, n * BANK + a:n * BANK + b]

        def blocks(ap):
            return ap.rearrange("p (b n) -> p b n", b=NB)

        RS_TAIL = 5 * BANK + 400

        with ExitStack() as over:
            y_tok = sb("y_tok", [P, TT, D], F32, over)
            y_smp = sb("y_smp", [NSEQ, D], F32, over)
        a_hi = sb("a_hi", [P, KT, T], F32R)
        a_lo = sb("a_lo", [P, KT, T], F32R)
        raw = [sb(f"raw{s}", [P, KT, P], F32) for s in range(2)]
        w_hi = [sb(f"w_hi{s}", [P, KT, P], F32R) for s in range(2)]
        w_lo = [sb(f"w_lo{s}", [P, KT, P], F32R) for s in range(2)]
        rinv = sb("rinv", [P, T], F32)
        ident = sb("ident", [P, P], F32)
        ones = sb("ones", [P, P], F32)
        vecs = sb("vecs", [P, KT, 24], F32)
        o_smp = sb("o_smp", [P, KT, NSEQ], F32)
        eps = sb("eps", [P, 1], F32)

        att = ExitStack()
        s_bias = sb("s_bias", [P, H, NPAGES], F32, att)
        s_new = sb("s_new", [P, NSEQ, H], F32, att)
        negcum = sb("negcum", [P, S], F32R, att)
        v_s = sb("v_s", [NSEQ, D], F32, att)
        ident_b = sb("ident_b", [P, P], BF16, att)
        mask_b = sb("mask_b", [P, P], BF16, att)
        sel_id = sb("sel_id", [P, H], F32, att)
        zeros = sb("zeros", [P, P], F32, att)
        pages_sb = sb("pages_sb", [1, NPAGES], I32, att)
        with ExitStack() as front:
            xtok = sb("xtok", [P, TT, D], F32, front)
            xsmp = sb("xsmp", [NSEQ, D], F32, front)
            vrow = sb("vrow", [24, D], F32, front)
            xf = [sb(f"xf{s}", [P, T], F32, front) for s in range(3)]
            sqt = [sb(f"sqt{n}", [P, T], F32, front) for n in range(2)]
            sqs0 = sb("sqs0", [P, T], F32, front)
            hs = sb("hs", [P, KT, NSEQ], F32, front)
            small = sb("small", [P, 8], F32, front)
            bf_col = sb("bf_col", [H, 1], F32, front)
            wseg = [sb(f"wseg{s}", [P, KT, 256], F32, front) for s in range(3)]
            q_s = sb("q_s", [NSEQ, D], F32, front)
            k_s = sb("k_s", [NSEQ, D], F32, front)
            lt = sb("lt", [P, (TT + 1) * H], F32, front)
            page_col = sb("page_col", [P, 1], I32, front)
            suffix = sb("suffix", [P, P], F32, front)
            owner = sb("owner", [NSEQ, P], F32, front)
            tot = sb("tot", [P, H], F32, front)
            snew_row = sb("snew_row", [NSEQ, H], F32, front)
            negd = sb("negd", [NSEQ, NSEQ], F32, front)
            mask_f = sb("mask_f", [P, P], F32, front)
        with ExitStack() as front2:
            lf = sb("lf", [P, PAGE * H], F32, front2)
            lc = sb("lc", [P, PAGE * H], F32, front2)
            gz = sb("gz", [H, T], F32, front2)
            ge = sb("ge", [H, T], F32, front2)
            gw = sb("gw", [H, T], F32, front2)
            gd = sb("gd", [H, T], F32, front2)
        with ExitStack() as loop:
            q_hi = sb("q_hi", [P, S], F32R, loop)
            q_lo = sb("q_lo", [P, S], F32R, loop)
            k_hi = sb("k_hi", [P, S], F32R, loop)
            k_lo = sb("k_lo", [P, S], F32R, loop)
            qv_raw = sb("qv_raw", [P, T], F32, loop)
            k_raw = sb("k_raw", [P, T], F32, loop)
            k_tok = sb("k_tok", [P, TT, P], F32, loop)
            v_tok = sb("v_tok", [P, TT, P], F32, loop)
            v_pack = sb("v_pack", [P, TT, 2, 2, DH], F32R, loop)
            probs = [sb(f"probs{n}", [P, S], F32, loop) for n in range(4)]
            pt_hi = [sb(f"pt_hi{n}", [P, BANK], F32R, loop) for n in range(2)]
            pt_lo = [sb(f"pt_lo{n}", [P, BANK], F32R, loop) for n in range(2)]
            sel = [sb(f"sel{h}", [P, P], F32R, loop) for h in range(2)]
            kpage = sb("kpage", [P, KSLOT, D], F32, loop)
            vpage = sb("vpage", [P, VSLOT, D], F32, loop)
            q_bc = sb("q_bc", [P, D], F32, loop)
            o_pair = sb("o_pair", [P, S], F32, loop)
            o_tmp = sb("o_tmp", [P, 256], F32, loop)
            nmax = sb("nmax", [P, 16], F32, loop)
            lsum = sb("lsum", [P, 16], F32, loop)
            s_raw = sb("s_raw", [P, NPG, H], F32, loop)
            z = sb("z", [P, NPG + 1, H], F32, loop)
            ps = sb("ps", [P, NPG + 1, H], F32, loop)
            zmax = sb("zmax", [P, H], F32, loop)
            mcol = sb("mcol", [H, 1], F32, loop)
            mdiag = sb("mdiag", [H, H], F32, loop)
            psum_s = sb("psum_s", [P, H], F32, loop)
            rl = sb("rl", [P, 1], F32, loop)
            o_rows = sb("o_rows", [P, 256], F32, loop)
        att.close()

        x_res = sb("x_res", [P, KT, T], F32)
        b_hi = sb("b_hi", [P, KT, T], F32R)
        b_lo = sb("b_lo", [P, KT, T], F32R)
        t0 = sb("t0", [P, T], F32)
        t1 = sb("t1", [P, T], F32)
        t2 = sb("t2", [P, T + 2], F32)
        t3 = sb("t3", [P, T], F32)
        conv_rows = sb("conv_rows", [P, KT, 2 + NSEQ], F32)
        smp_g = sb("smp_g", [P, KT, NSEQ], F32)
        r_col = sb("r_col", [P, TT + 1], F32)

        w_raw = [sem(f"w_raw{s}") for s in range(2)]
        w_hid = [sem(f"w_hid{s}") for s in range(2)]
        w_lod = [sem(f"w_lod{s}") for s in range(2)]
        mm = [sem(f"mm{s}") for s in range(2)]
        ev = [sem(f"ev{s}") for s in range(2)]
        dv = sem("dv")
        ac = sem("ac")
        po = sem("po")
        cst = sem("cst")
        cst_b = sem("cst_b")
        x_in = sem("x_in")
        x_c = [sem(f"x_c{c}") for c in range(KT // 2)]
        vrow_in = sem("vrow_in")
        misc_in = sem("misc_in")
        lf_in = sem("lf_in")
        vec_t = sem("vec_t")
        vec_d = sem("vec_d")
        ftr = sem("ftr")
        fev = sem("fev")
        xsp = [sem(f"xsp{s}") for s in range(3)]
        ahi = sem("ahi")
        alo = sem("alo")
        sqr = sem("sqr")
        sqa = sem("sqa")
        rs = sem("rs")
        rq = sem("rq")
        rr = sem("rr")
        fz = sem("fz")
        fa = sem("fa")
        lgt_in = sem("lgt_in")
        lgt = sem("lgt")
        lgo = sem("lgo")
        out0 = sem("out0")
        rsm = sem("rsm")
        hsd = sem("hsd")
        wsg = [sem(f"wsg{s}") for s in range(3)]
        smm = sem("smm")
        sme = sem("sme")
        qsp = sem("qsp")
        lct = sem("lct")
        lco = sem("lco")
        lcb = sem("lcb")
        lbt = sem("lbt")
        lbe = sem("lbe")
        ready = sem("ready")
        qkv_h = sem("qkv_h")
        qkv_l = sem("qkv_l")
        tkt = sem("tkt")
        tke = sem("tke")
        vtk = sem("vtk")
        tkl = sem("tkl")
        ktd = sem("ktd")
        vtd = sem("vtd")
        seld = sem("seld")
        sd = sem("sd")
        mxd = sem("mxd")
        exd = sem("exd")
        pnd = sem("pnd")
        ptd = sem("ptd")
        pth = sem("pth")
        ptl = sem("ptl")
        pvd = sem("pvd")
        ocp = sem("ocp")
        oad = sem("oad")
        osp = sem("osp")
        kin = [sem(f"kin{n}") for n in range(KSLOT)]
        vin = [sem(f"vin{n}") for n in range(VSLOT)]
        lin = [sem(f"lin{n}") for n in range(KSLOT + VSLOT)]
        qbi = sem("qbi")
        kml = sem("kml")
        kfr = sem("kfr")
        vfr = sem("vfr")
        sa1 = sem("sa1")
        sa2 = sem("sa2")
        sa3 = sem("sa3")
        sa4 = sem("sa4")
        sa5 = sem("sa5")
        sa6 = sem("sa6")
        sa7 = sem("sa7")
        sa8 = sem("sa8")
        so1 = sem("so1")
        so2 = sem("so2")
        sa9 = sem("sa9")
        oin = [sem(f"oin{s}") for s in range(4)]
        oas = sem("oas")
        bhi = sem("bhi")
        blo = sem("blo")
        xin = sem("xin")
        sil = sem("sil")
        prd = sem("prd")
        cvt = sem("cvt")
        cvp = sem("cvp")
        cvc = sem("cvc")
        yt = sem("yt")
        ytt = sem("ytt")
        yte = sem("yte")
        ysm = sem("ysm")
        yss = sem("yss")
        yrt = sem("yrt")
        yrc = sem("yrc")
        yrv = sem("yrv")
        yra = sem("yra")
        outs = sem("outs")

        NORMS = dict(mix0=0, mix1=1, ffn0=2, ffn1=3, final=4)
        TAP = 5
        PREV = 8
        POOL_K = (1, 2, 4, 5, 6, 7, 8, 9, 10, 11, 12, 13, 14, 15)
        KEYS_IN_PROJECTION = 8
        S_OUT, S_SUM, S_MAX, S_SPREAD = 0, 256, 272, 400
        HQ = H // 4

        def last_slot(g):
            n = g % (KSLOT + VSLOT)
            return (kpage[:, n, :] if n < KSLOT else vpage[:, n - KSLOT, :]), KSLOT + VSLOT

        def ctr(*sems):
            return [Count(s) for s in sems]

        block = ctx.enter_context(nc.Block())

        @block.sync
        def _(sp):
            def load_x(c):
                sp.dma_start(xtok[:, :, 2 * P * c:2 * P * (c + 1)], x_tok[:, :, 2 * P * c:2 * P * (c + 1)])\
                  .then_inc(x_c[c], 16)

            load_x(0)
            sp.dma_start(xsmp[:, :], x_smp).then_inc(x_in, 16)
            sp.dma_start(vrow[0:2, :], norm_mix).then_inc(vrow_in, 16)
            sp.dma_start(vrow[2:4, :], norm_ffn).then_inc(vrow_in, 16)
            sp.dma_start(vrow[4:5, :], norm_final.rearrange("(o d) -> o d", o=1)).then_inc(vrow_in, 16)
            sp.dma_start(vrow[TAP:TAP + 3, :], conv_kernel.rearrange("l j d -> (l j) d")).then_inc(vrow_in, 16)
            sp.dma_start(vrow[PREV:24, :], state_conv.rearrange("l b j d -> (l b j) d")).then_inc(vrow_in, 16)
            for c in range(1, KT // 2):
                load_x(c)
            sp.dma_start(pages_sb[:, :], page_table.rearrange("b (o g) -> o (b g)", o=1)).then_inc(misc_in, 16)
            sp.dma_start(page_col[:, :], page_table.rearrange("b (g o) -> (b g) o", o=1)).then_inc(misc_in, 16)
            sp.dma_start(bf_col[:, :], attn_b_f.rearrange("l (h o) -> (l h) o", o=1)).then_inc(misc_in, 16)

            wl = [Count(w_lod[s]) for s in range(2)]

            def load_w(s, src, kts=KT, cols=P, first=False):
                if not first:
                    sp.wait_ge(w_lod[s], wl[s].up())
                sp.dma_start(raw[s][:, 0:kts, 0:cols], src).then_inc(w_raw[s], 16)

            load_w(0, w_qkvf[:, 3 * D:3 * D + H].rearrange("(k p) c -> p k c", p=P), cols=H, first=True)
            load_w(1, w_tile(w_qkvf, 0, KT, D), first=True)
            NSEG = 3 * D // 256
            for m in range(KT):
                sp.wait_ge(fev, m + 1)
                sp.dma_start(x_spill[m, :, :], xf[m % 3][:, :]).then_inc(xsp[m % 3], 16)
            for n in range(NSEG):
                if n == 3:
                    load_w(0, w_tile(w_qkvf, 0, KT, 0))
                if n >= 3:
                    sp.wait_ge(smm, n - 2)
                sp.dma_start(wseg[n % 3][:, :, :],
                             w_qkvf[:, n * 256:(n + 1) * 256].rearrange("(k p) c -> p k c", p=P)).then_inc(wsg[n % 3], 16)
            sp.wait_ge(sme, NSEG)
            sp.dma_start(q_spill, q_s[:, :]).then_inc(qsp, 16)
            sp.dma_start(k_sample.rearrange("l b o h d -> (l b o) (h d)"), k_s[:, :]).then_inc(out0, 16)
            sp.dma_start(v_sample.rearrange("l b o h d -> (l b o) (h d)"), v_s[:, :]).then_inc(out0, 16)
            sp.wait_ge(lgo, 1)
            sp.dma_start(logf_prompt.rearrange("l o (t p) h -> p (l o t) h", p=P),
                         lt[:, 0:TT * H].rearrange("p (t h) -> p t h", h=H)).then_inc(out0, 16)
            sp.dma_start(logf_sample.rearrange("l b o h -> (l b o) h"),
                         lt[0:NSEQ, TT * H:(TT + 1) * H]).then_inc(out0, 16)
            sp.wait_ge(ready, 1)
            sp.wait_ge(out0, 64)
            sp.wait_ge(qsp, 16)
            for n in range(3):
                sp.wait_ge(xsp[n], 16 * len(range(n, KT, 3)))
            sp.wait_ge(misc_in, 48)

            kf, vf = ctr(kfr, vfr)

            def page_id(n):
                return sp.value_load(pages_sb[0:1, bass.ds(n, 1)], min_val=0, max_val=POOL - 1)

            def load_k(i, g, fresh):
                if not fresh:
                    sp.wait_ge(kfr, kf.up())
                src = k_pages[bass.ds(page_id(i * NPG + g), 1), :, :].rearrange("a p n -> p (a n)")
                sp.dma_start(kpage[:, g % KSLOT, :], src).then_inc(kin[g % KSLOT], 16)

            def load_v(b, g, fresh):
                if not fresh:
                    sp.wait_ge(vfr, vf.up())
                src = v_pages[bass.ds(page_id(b * NPG + g), 1), :, :].rearrange("a p n -> p (a n)")
                sp.dma_start(vpage[:, g % VSLOT, :], src).then_inc(vin[g % VSLOT], 16)

            def pair(i, first=False, v_fresh=False, last=False):
                if first:
                    sp.dma_start(q_bc[:, :], q_spill[0:1, :].to_broadcast([P, D])).then_inc(qbi, 16)
                load_w(0, w_tile(w_qkvf, 0, KT, i * P + 2 * D))
                if not first:
                    sp.wait_ge(kfr, kf.value + KSLOT)
                    sp.dma_start(q_bc[:, :], q_spill[bass.ds(i, 1), :].to_broadcast([P, D])).then_inc(qbi, 16)
                for g in range(KEYS_IN_PROJECTION):
                    load_k(i, g, first and g < KSLOT)
                    if g == 3 and not first:
                        load_v(i - 1, 0, v_fresh)
                        load_v(i - 1, 1, v_fresh)
                def values(*pages):
                    for g in pages:
                        if not first:
                            load_v(i - 1, g, False)

                for g in range(KEYS_IN_PROJECTION, KEYS_IN_PROJECTION + KSLOT):
                    load_k(i, g, False)
                values(2, 3)
                load_w(1, w_tile(w_o, 0, KT, P) if last else w_tile(w_qkvf, 0, KT, i * P + (P + D)))
                load_k(i, 12, False)
                load_k(i, 13, False)
                values(4, 5)
                load_k(i, 14, False)
                values(6, 7)
                load_k(i, 15, False)
                values(8)
                load_w(0, w_tile(w_o, 0, KT, 0) if last else w_tile(w_qkvf, 0, KT, i * P + P))
                values(*range(9, NPG))

            pair(0, first=True)
            pair(1, v_fresh=True)
            with counted_loop(sp, 2, NPAIR - 1, {wl[0]: 2, wl[1]: 1, kf: 16, vf: 16}) as i:
                pair(i)
            pair(NPAIR - 1, last=True)
            for g in range(NPG):
                slot, n_slots = last_slot(g)
                if g < KSLOT:
                    sp.wait_ge(kfr, NPAGES - KSLOT + g + 1)
                elif g < n_slots:
                    sp.wait_ge(vfr, NPAGES - NPG - n_slots + g + 1)
                else:
                    sp.wait_ge(vfr, NPAGES - NPG + g - n_slots + 1)
                src = v_pages[bass.ds(page_id((NSEQ - 1) * NPG + g), 1), :, :].rearrange("a p n -> p (a n)")
                sp.dma_start(slot, src).then_inc(lin[g % n_slots], 16)

            sp.wait_ge(osp, 16 * NPAIR)
            sp.wait_ge(sa9, NSEQ)
            sp.wait_ge(ktd, 16 * NPAIR)
            sp.wait_ge(vtd, 16 * NPAIR)
            for m in range(KT):
                if m >= 4:
                    sp.wait_ge(blo, m - 3)
                sp.dma_start((t0, t1, t2, t3)[m % 4][:, 0:S], o_spill[m, :, :]).then_inc(oin[m % 4], 16)
            sp.dma_start(x_res[:, :, :], x_spill.rearrange("k p t -> p k t")).then_inc(xin, 16)

            def out_loads(w, row, kts, first_pair=0):
                with counted_loop(sp, first_pair, KT // 2, {wl[0]: 1, wl[1]: 1}) as i:
                    load_w(0, w_tile(w, row, kts, i * (2 * P)), kts)
                    load_w(1, w_tile(w, row, kts, i * (2 * P) + P), kts)

            def ffn_loads(l):
                h0 = 0
                for n in CHUNKS:
                    with counted_loop(sp, 0, n, {wl[0]: 1, wl[1]: 1}) as j:
                        load_w(0, w_tile(w_in[l], 0, KT, j * P + h0 * P))
                        load_w(1, w_tile(w_in[l], 0, KT, j * P + (h0 * P + DFF)))
                    out_loads(w_out[l], h0 * P, n)
                    h0 += n

            out_loads(w_o, 0, KT, first_pair=1)
            ffn_loads(0)
            with counted_loop(sp, 0, KT // 2, {wl[0]: 3, wl[1]: 3}) as i:
                for m in range(2):
                    for r in range(3):
                        load_w((3 * m + r) % 2, w_tile(w_cin, 0, KT, i * (2 * P) + (m * P + r * D)))
            out_loads(w_cout, 0, KT)
            ffn_loads(1)
            for t in range(TT):
                sp.wait_ge((yrv, yra)[t % 2], t // 2 + 1)
                sp.dma_start(y_prompt.rearrange("o (t p) d -> p (o t) d", p=P)[:, t, :], y_tok[:, t, :]).then_inc(outs, 16)
            sp.wait_ge(yrv, TT // 2 + 1)
            sp.dma_start(y_sample.rearrange("b o d -> (b o) d"), y_smp[:, :]).then_inc(outs, 16)
            sp.dma_start(conv_sample[0, :, 0, :], state_conv[0, :, 1, :]).then_inc(outs, 16)
            sp.wait_ge(outs, 16 * (TT + 2 + 2))

        @block.gpsimd
        def _(gp):
            def own(ins, sem_=po):
                ins.then_inc(sem_, 1)

            steps = Count(po)

            def then(ins):
                ins.then_inc(po, 1)
                gp.wait_ge(po, steps.up())

            gp.memset(eps[:, :], RMS_EPS)
            then(gp.memset(ones[:, :], 1.0))
            gp.affine_select(out=ident[:, :], in_=ones[:, :], compare_op=ALU.is_equal, fill=0.0, base=0,
                             pattern=[[-1, P]], channel_multiplier=1).then_inc(cst, 1)
            then(gp.memset(mask_f[:, :], 0.0))
            gp.affine_select(out=mask_f[:, :], in_=mask_f[:, :], compare_op=ALU.is_ge, fill=NEG_INF, base=0,
                             pattern=[[-1, P]], channel_multiplier=1).then_inc(cst, 1)
            then(gp.affine_select(out=suffix[:, :], in_=ones[:, :], compare_op=ALU.is_ge, fill=0.0, base=0,
                                  pattern=[[-1, P]], channel_multiplier=1))
            then(gp.affine_select(out=suffix[:, :], in_=suffix[:, :], compare_op=ALU.is_ge, fill=0.0, base=NPG - 1,
                                  pattern=[[NPG, NSEQ], [0, NPG]], channel_multiplier=-1))
            then(gp.affine_select(out=owner[:, :], in_=ones[0:NSEQ, :], compare_op=ALU.is_ge, fill=0.0, base=0,
                                  pattern=[[1, P]], channel_multiplier=-NPG))
            gp.affine_select(out=owner[:, :], in_=owner[:, :], compare_op=ALU.is_ge, fill=0.0, base=NPG - 1,
                             pattern=[[-1, P]], channel_multiplier=NPG).then_inc(cst, 1)
            then(gp.memset(sel_id[:, :], 0.0))
            for q in range(4):
                ins = gp.affine_select(out=sel_id[:, :], in_=sel_id[:, :], compare_op=ALU.not_equal, fill=1.0,
                                       base=-32 * q, pattern=[[-1, H]], channel_multiplier=1)
                if q < 3:
                    then(ins)
                else:
                    ins.then_inc(cst, 1)
            gp.memset(s_new[:, :, :], NEG_INF)
            gp.memset(zeros[:, :], 0.0).then_inc(cst, 1)
            gp.memset(negcum[:, :].bitcast(F32), 0.0).then_inc(cst, 1)
            gp.memset(w_hi[0][:, :, :].bitcast(F32), 0.0).then_inc(cst, 1)
            gp.wait_ge(misc_in, 48)

            wh = [Count(w_hid[s]) for s in range(2)]
            sq = Count(sqr)

            def low(s, kts=KT, cols=P):
                gp.wait_ge(w_hid[s], wh[s].up())
                gp.tensor_tensor(w_lo[s][:, 0:kts, 0:cols], raw[s][:, 0:kts, 0:cols],
                                 w_hi[s][:, 0:kts, 0:cols].bitcast(F32), ALU.subtract).then_inc(w_lod[s], 1)

            sums = Count(sqa)

            def add_squares(total, tile, first=False):
                gp.wait_ge(sqr, sq.up())
                if not first:
                    gp.wait_ge(sqa, sums.value)
                gp.tensor_tensor(total, total, tile, ALU.add).then_inc(sqa, 1)
                sums.up()

            then(gp.memset(sqs0[:, :], 0.0))
            then(gp.memset(w_lo[0][:, :, :].bitcast(F32), 0.0))
            for m in range(KT):
                add_squares(sqs0[:, :], sqt[m % 2][:, :], first=m == 0)
                if m == 0:
                    low(0, cols=H)
                    low(1)
            gp.wait_ge(ftr, KT)
            gp.wait_ge(vec_t, 1)
            gp.indirect_dma_start(out=lf[:, :], out_offset=None, in_=logf_pages,
                                  in_offset=bass.IndirectOffsetOnAxis(ap=page_col[:, 0:1], axis=0)).then_inc(lf_in, 16)
            low(0)
            gp.wait_ge(ready, 1)

            kp = [Count(kin[n], 16) for n in range(KSLOT)]
            qb = Count(qbi, 16)

            def multiply(g):
                kp[g % KSLOT].up()
                if g in POOL_K:
                    gp.wait_ge(kin[g % KSLOT], kp[g % KSLOT].value)
                    gp.tensor_tensor(kpage[:, g % KSLOT, :], kpage[:, g % KSLOT, :], q_bc[:, :], ALU.mult)\
                      .then_inc(kml, 1)

            vl, vd = Count(tkl), Count(vtd, 16)

            def pair(first):
                gp.wait_ge(qbi, qb.up())
                for g in range(4):
                    multiply(g)
                low(0)
                for g in range(4, KEYS_IN_PROJECTION):
                    multiply(g)
                for n in range(8):
                    multiply(KEYS_IN_PROJECTION + n)
                    if n == 2:
                        low(1)
                    if n == 3:
                        vl.up()
                        gp.wait_ge(tkl, vl.up())
                        if not first:
                            gp.wait_ge(vtd, vd.up())
                        gp.tensor_tensor(v_tok[:, :, :].rearrange("p t (h d) -> p t h d", d=DH),
                                         v_pack[:, :, :, 0, :].bitcast(F32), v_pack[:, :, :, 1, :].bitcast(F32),
                                         ALU.add).then_inc(vtk, 1)
                    if n == 6:
                        low(0)

            pair(True)
            with counted_loop(gp, 1, NPAIR, {qb: 1, wh[0]: 2, wh[1]: 1, vl: 2, vd: 1,
                                             **{kp[n]: 4 for n in range(KSLOT)}}) as i:
                pair(False)

            z3 = t2[:, 0:T]
            rsc = Count(rs)

            def out_lows(last=False, final=False):
                def turn(more=True):
                    for s in range(2):
                        if more:
                            low(s)
                        if final:
                            add_squares(z3, t3[:, :])
                if final:
                    gp.wait_ge(rs, rsc.up())
                    then(gp.memset(z3, 0.0))
                per = {wh[0]: 1, wh[1]: 1}
                if final:
                    per |= {sq: 2, sums: 2}
                with counted_loop(gp, 0, KT // 2 - (1 if last else 0), per) as i:
                    turn()
                if last:
                    turn(False)

            hi_c = Count(bhi)

            def ffn_lows(last):
                for c, n in enumerate(CHUNKS):
                    with counted_loop(gp, 0, n, {wh[0]: 1, wh[1]: 1, hi_c: 1}) as j:
                        low(0)
                        low(1)
                        gp.wait_ge(bhi, hi_c.up())
                        gp.tensor_tensor(b_lo[:, bass.ds(j, 1), :].rearrange("p a t -> p (a t)"), t1[:, :],
                                         b_hi[:, bass.ds(j, 1), :].rearrange("p a t -> p (a t)").bitcast(F32),
                                         ALU.subtract).then_inc(blo, 1)
                    end = c == len(CHUNKS) - 1
                    out_lows(last=last and end, final=end)

            hi_c.value = KT
            gp.wait_ge(oad, 8 * NPAIR)
            gp.wait_ge(sa9, NSEQ)
            gp.wait_ge(blo, KT)
            out_lows(final=True)
            ffn_lows(False)
            with counted_loop(gp, 0, KT // 2, {wh[0]: 3, wh[1]: 3}) as i:
                for r in range(6):
                    low(r % 2)
            hi_c.value = hi_c.value + KT
            gp.wait_ge(blo, hi_c.value)
            out_lows(final=True)
            ffn_lows(True)

        @block.scalar
        def _(act):
            wr = [Count(w_raw[s], 16) for s in range(2)]
            done = [Count(mm[s]) for s in range(2)]
            evc = [Count(ev[s]) for s in range(2)]
            steps = Count(ac)

            def then(ins):
                ins.then_inc(ac, 1)
                act.wait_ge(ac, steps.up())

            def high(s, cols=P, fresh=False):
                act.wait_ge(w_raw[s], wr[s].up())
                if not fresh:
                    act.wait_ge(mm[s], done[s].up())
                act.activation(w_hi[s][:, :, 0:cols], raw[s][:, :, 0:cols], ACT.Copy).then_inc(w_hid[s], 1)

            act.wait_ge(x_in, 16)
            act.wait_ge(cst, 7)
            then(act.activation(sqt[0][0:NSEQ, 0:D], xsmp[:, :], ACT.Square, accum_out=small[0:NSEQ, 0:1]))
            act.activation(small[0:NSEQ, 1:2], small[0:NSEQ, 0:1], ACT.Sqrt, bias=eps[0:NSEQ, :],
                           scale=1.0 / D).then_inc(rsm, 1)

            sa, fe, rd = ctr(sqa, fev, rs)

            def normed(m, x, norm, square_to):
                act.activation(a_hi[:, m, :] if isinstance(m, int) else
                               a_hi[:, bass.ds(m, 1), :].rearrange("p a t -> p (a t)"),
                               x, ACT.Copy, scale=vecs[:, m, NORMS[norm]:NORMS[norm] + 1] if isinstance(m, int) else
                               vecs[:, bass.ds(m, 1), NORMS[norm]:NORMS[norm] + 1].rearrange("p a o -> p (a o)"))\
                   .then_inc(ahi, 1)
                squares(x, square_to)

            def squares_free():
                act.wait_ge(sqa, sa.value)

            def squares(x, square_to):
                act.activation(square_to, x, ACT.Square).then_inc(sqr, 1)
                sa.up()

            def roots():
                act.wait_ge(rs, rd.up())
                act.activation(rinv[:, S:T], PS[:, RS_TAIL:RS_TAIL + NSEQ], ACT.Sqrt, bias=eps[:, :],
                               scale=1.0 / D).then_inc(rq, 1)
                act.activation(rinv[:, 0:S], PS[:, 6 * BANK:8 * BANK], ACT.Sqrt, bias=eps[:, :],
                               scale=1.0 / D).then_inc(rq, 1)

            act.wait_ge(vec_d, 1)
            for m in range(KT):
                if m >= 2:
                    act.wait_ge(sqa, m - 1)
                act.wait_ge(fev, fe.up())
                normed(m, xf[m % 3][:, :], "mix0", sqt[m % 2][:, :])
                if m == 0:
                    high(0, cols=H, fresh=True)
                    high(1, fresh=True)
            roots()
            high(0)
            act.wait_ge(fz, 1)
            then(act.activation(ge[:, :], gz[:, :], ACT.Abs))
            act.activation(ge[:, :], ge[:, :], ACT.Exp, scale=-1.0).then_inc(fa, 1)
            act.wait_ge(fz, 2)
            act.activation(gd[:, :], gw[:, :], ACT.Ln).then_inc(fa, 1)
            act.wait_ge(ready, 1)
            evc[0].up()

            tk, sdc, ptc, mx, pn, pv, s5, oac, kd, vk = ctr(tkt, sd, ptd, mxd, pnd, pvd, sa5, oad, ktd, vtk)
            kd.step = 16
            ow = Count(osp, 16)
            plc = Count(ptl)

            def pair(i, first=False, sample=True):
                high(0)
                act.wait_ge(ev[0], evc[0].up())
                act.activation(q_hi[:, :], qv_raw[:, 0:S], ACT.Copy).then_inc(qkv_h, 1)
                act.wait_ge(ev[1], evc[1].up())
                act.activation(k_hi[:, :], k_raw[:, 0:S], ACT.Copy).then_inc(qkv_h, 1)
                evc[0].up()
                if sample:
                    act.wait_ge(sa5, s5.up())
                    act.activation(ps[:, :, :], z[:, :, :], ACT.Exp).then_inc(sa6, 1)
                if not first:
                    act.wait_ge(ktd, kd.up())
                for n in range(2):
                    act.wait_ge(tkt, tk.up())
                    act.activation(k_tok[:, 4 * n:4 * n + 4, :], bank(4 + n).rearrange("p (t c) -> p t c", c=P),
                                   ACT.Copy).then_inc(tke, 1)
                    then_count()
                act.wait_ge(tke, tkv.value)
                act.dma_start(k_out[:, :, bass.ds(i * P, P)], k_tok[:, :, :]).then_inc(ktd, 16)
                slot = [0]

                def exponentials(n, t):
                    h, jj = n // 4, n % 4
                    t += 2 * jj
                    k = 8 * h + t
                    w = P * (t + 1)
                    act.wait_ge(mxd, mx.up())
                    act.activation(probs[(n % 2) * 2 + t % 2][:, 0:w],
                                   PS[:, 2 * (t % 2) * BANK:2 * (t % 2) * BANK + w], ACT.Exp,
                                   bias=nmax[:, k:k + 1], accum_out=lsum[:, k:k + 1]).then_inc(exd, 1)

                def v_rows():
                    for n in range(2):
                        act.wait_ge(tkt, tk.up())
                        act.activation(v_pack[:, 4 * n:4 * n + 4, :, 0, :],
                                       bank(4 + n).rearrange("p (t h c) -> p t h c", h=2, c=DH), ACT.Copy).then_inc(tke, 1)
                        then_count()

                def high_transposed(g, n):
                    act.wait_ge(ptd, ptc.up())
                    if not (first and n <= 2 and g == 0):
                        act.wait_ge(pvd, pv.up())
                    act.activation(pt_hi[slot[0] % 2][:, :], bank(4 + slot[0] % 2), ACT.Copy).then_inc(pth, 1)
                    slot[0] += 1

                def output_half(n):
                    h, jj = n // 4, n % 4
                    for _ in range(jj + 1):
                        opd.up()
                    act.wait_ge(pvd, opd.value)
                    if not (first and n == 0):
                        act.wait_ge(oad, oac.up())
                    rows = (P - DH, P) if h == 0 else (0, DH)
                    act.activation(o_tmp[h * DH:(h + 1) * DH, :], PS[rows[0]:rows[1], 6 * BANK:6 * BANK + 256],
                                   ACT.Copy).then_inc(ocp, 1)

                for n in range(10):
                    if n == 4:
                        act.wait_ge(vtk, vk.up())
                        act.dma_start(v_out[:, :, bass.ds(i * P, P)], v_tok[:, :, :]).then_inc(vtd, 16)
                    if n == 1:
                        v_rows()
                    if n < 8:
                        exponentials(n, 0)
                    if n >= 2:
                        output_half(n - 2)
                    groups = (n - 1) % 4 + 1 if 0 < n < 9 else 0
                    for g in range(min(3, groups)):
                        high_transposed(g, n)
                    if n < 8:
                        exponentials(n, 1)
                    if groups == 4:
                        high_transposed(3, n)
                    if n == 1:
                        high(1)
                    if n == 5:
                        high(0)
                act.wait_ge(oad, oac.value + 1)
                act.dma_start(o_spill[bass.ds(i, 1), :, :].rearrange("a p t -> p (a t)"), o_pair[:, :]).then_inc(osp, 16)

            tkv = Count(tke)

            def then_count():
                tkv.up()

            opd = Count(pvd)
            pair(0, first=True, sample=False)
            with counted_loop(act, 1, NPAIR, {wr[0]: 2, wr[1]: 1, done[0]: 2, done[1]: 1, evc[0]: 2, evc[1]: 1, tk: 4, tkv: 4,
                                              mx: 16, ptc: 20, pv: 20, oac: 8, kd: 1, vk: 1, s5: 1,
                                              opd: 20}) as i:
                pair(i)
            act.wait_ge(sa5, s5.up())
            act.activation(ps[:, :, :], z[:, :, :], ACT.Exp).then_inc(sa6, 1)

            oc = Count(oas)
            for m in range(KT):
                act.wait_ge(oas, oc.up())
                act.activation(b_hi[:, m, :], (t0, t1, t2, t3)[m % 4][:, 0:T], ACT.Copy).then_inc(bhi, 1)

            def tile(t, m):
                return t[:, bass.ds(m, 1), :].rearrange("p a t -> p (a t)")

            def rows_out(m):
                act.wait_ge(ytt, m + 1)
                act.activation(y_tok[:, :, m * P:(m + 1) * P],
                               PS[:, 6 * BANK:8 * BANK].rearrange("p (t c) -> p t c", c=P), ACT.Copy).then_inc(yte, 1)

            def final_highs():
                for m in range(KT):
                    s = m % 2
                    if m < KT - 2:
                        high(s)
                    squares_free()
                    act.wait_ge(ev[s], evc[s].up())
                    squares(x_res[:, m, :], t3[:, :])
                    if m > 0:
                        rows_out(m - 1)
                rows_out(KT - 1)
                act.wait_ge(yss, 1)
                act.activation(r_col[:, 0:TT], bank(3, 0, TT), ACT.Sqrt, bias=eps[:, :], scale=1.0 / D)
                act.activation(r_col[0:NSEQ, TT:TT + 1], PS[0:NSEQ, 3 * BANK + TT:3 * BANK + TT + 1], ACT.Sqrt,
                               bias=eps[0:NSEQ, :], scale=1.0 / D).then_inc(yrt, 1)
                act.wait_ge(yrc, 1)
                act.wait_ge(yte, KT)
                for t in range(1, TT, 2):
                    act.activation(y_tok[:, t, :], y_tok[:, t, :], ACT.Copy, scale=r_col[:, t:t + 1]).then_inc(yra, 1)

            def out_highs(norm):
                def turn(i):
                    for s in range(2):
                        high(s)
                        if norm:
                            squares_free()
                            act.wait_ge(ev[s], evc[s].up())
                            normed(2 * i + s, tile(x_res, 2 * i + s), norm, t3[:, :])
                        else:
                            evc[s].up()
                per = {wr[0]: 1, wr[1]: 1, done[0]: 1, done[1]: 1, evc[0]: 1, evc[1]: 1}
                if norm:
                    per[sa] = 2
                with counted_loop(act, 0, KT // 2, per) as i:
                    turn(i)
                if norm:
                    roots()

            pr = Count(prd)

            def ffn_highs(norm):
                for c, n in enumerate(CHUNKS):
                    with counted_loop(act, 0, n, {wr[0]: 1, wr[1]: 1, done[0]: 1, done[1]: 1, evc[0]: 1, evc[1]: 1,
                                                  pr: 1}) as j:
                        high(0)
                        act.wait_ge(ev[0], evc[0].up())
                        act.activation(t0[:, :], t0[:, :], ACT.Silu).then_inc(sil, 1)
                        high(1)
                        evc[1].up()
                        act.wait_ge(prd, pr.up())
                        act.activation(tile(b_hi, j), t1[:, :], ACT.Copy).then_inc(bhi, 1)
                    end = c == len(CHUNKS) - 1
                    if end and norm == "final":
                        final_highs()
                    else:
                        out_highs(norm if end else None)

            out_highs("ffn0")
            ffn_highs("mix1")
            with counted_loop(act, 0, KT // 2, {wr[0]: 3, wr[1]: 3, done[0]: 3, done[1]: 3, evc[0]: 3, evc[1]: 3,
                                                pr: 2}) as i:
                for r in range(6):
                    high(r % 2)
                    evc[r % 2].up()
                    if r % 3 == 2:
                        act.wait_ge(prd, pr.up())
                        act.activation(tile(b_hi, 2 * i + r // 3), t3[:, :], ACT.Copy).then_inc(bhi, 1)
            for n in range(2):
                act.wait_ge(cvp, 1)
                act.activation(t0[0:2 + NSEQ, n * BANK:(n + 1) * BANK], PS[0:2 + NSEQ, (6 + n) * BANK:(7 + n) * BANK],
                               ACT.Copy).then_inc(cvc, 1)
            act.wait_ge(cvc, 2)
            act.dma_start(conv_prompt.rearrange("l o j d -> (l o j) d"), t0[0:2, 0:D]).then_inc(outs, 16)
            act.dma_start(conv_sample[0, :, 1, :], t0[2:2 + NSEQ, 0:D]).then_inc(outs, 16)
            act.wait_ge(outs, 32)
            out_highs("ffn1")
            ffn_highs("final")

        @block.tensor
        def _(pe):
            wlo = [Count(w_lod[s]) for s in range(2)]
            evd = [Count(ev[s]) for s in range(2)]

            def product(s, hi, lo, kts=KT, fresh=False, parts=None):
                open_product(s, fresh)
                product_steps(s, hi, lo, range(kts), kts, parts)

            def open_product(s, fresh=False):
                pe.wait_ge(w_lod[s], wlo[s].up())
                if not fresh:
                    pe.wait_ge(ev[s], evd[s].up())

            def product_steps(s, hi, lo, ks, kts=KT, parts=None):
                g = group(s)
                for k in ks:
                    if parts:
                        pe.wait_ge(parts.sem, parts.up())
                    for n, (w, x) in enumerate(((w_hi[s], hi), (w_hi[s], lo), (w_lo[s], hi))):
                        for b in range(NB):
                            ins = pe.matmul(g[:, b, :], w[:, k, :], x[:, k, b * TB:(b + 1) * TB],
                                            start=k == 0 and n == 0, stop=k == kts - 1 and n == 2)
                if ks[-1] == kts - 1:
                    ins.then_inc(mm[s], 1)

            pe.wait_ge(cst, 7)
            pe.wait_ge(vrow_in, 80)
            for k in range(KT):
                ins = pe.transpose(PS[:, 6 * BANK + 24 * k:6 * BANK + 24 * (k + 1)], vrow[:, k * P:(k + 1) * P],
                                   ident[0:24, 0:24])
            ins.then_inc(vec_t, 1)
            pe.wait_ge(x_in, 16)
            for k in range(KT):
                s = k % 2
                if k % 2 == 0:
                    pe.wait_ge(x_c[k // 2], 16)
                if k >= 2:
                    pe.wait_ge(fev, k - 1)
                base = 3 * s * BANK
                for t in range(TT):
                    pe.transpose(PS[:, base + t * P:base + (t + 1) * P], xtok[:, t, k * P:(k + 1) * P], ident[:, :])
                pe.transpose(PS[:, base + S:base + T], xsmp[:, k * P:(k + 1) * P], ident[0:NSEQ, 0:NSEQ])\
                  .then_inc(ftr, 1)

            sq = Count(sqa)

            def sum_squares(total):
                for _ in range(KT):
                    sq.up()
                pe.wait_ge(sqa, sq.value)
                pe.matmul(bank(6), ones[:, :], total[:, 0:BANK], start=True, stop=True)
                pe.matmul(bank(7), ones[:, :], total[:, BANK:S], start=True, stop=True)
                pe.matmul(PS[:, RS_TAIL:RS_TAIL + NSEQ], ones[:, :], total[:, S:T], start=True, stop=True)\
                  .then_inc(rs, 1)

            lo_parts = Count(alo)
            pe.wait_ge(fev, KT)
            product(0, a_hi, a_lo, fresh=True, parts=lo_parts)
            pe.wait_ge(vec_d, 1)
            sum_squares(sqs0)

            def gate_rows():
                pe.wait_ge(lgt_in, 1)
                for t in range(TT):
                    pe.transpose(bank(3, t * H, (t + 1) * H), gz[:, t * P:(t + 1) * P], ident[0:H, 0:H])
                pe.transpose(PS[0:NSEQ, 3 * BANK + TT * H:3 * BANK + (TT + 1) * H], gz[:, S:T], ident[0:H, 0:H])\
                  .then_inc(lgt, 1)

            def page_sums():
                pe.wait_ge(lct, 1)
                pe.wait_ge(lgo, 1)
                pe.matmul(bank(4, 0, H), suffix[:, :], tot[:, :], start=True, stop=False)
                pe.matmul(bank(4, 0, H), owner[:, :], lt[0:NSEQ, TT * H:(TT + 1) * H], start=False, stop=True)\
                  .then_inc(lco, 1)

            pe.wait_ge(hsd, 1)
            pe.wait_ge(rq, 2)
            for n in range(3 * D // 256):
                pe.wait_ge(wsg[n % 3], 16 * (n // 3 + 1))
                if n >= 2:
                    pe.wait_ge(sme, n - 1)
                for k in range(KT):
                    ins = pe.matmul(PS[0:NSEQ, (6 + n % 2) * BANK:(6 + n % 2) * BANK + 256], hs[:, k, :],
                                    wseg[n % 3][:, k, :], start=k == 0, stop=k == KT - 1)
                ins.then_inc(smm, 1)
                if n == 8:
                    gate_rows()
                if n == 10:
                    page_sums()
            pe.wait_ge(lcb, 1)
            for h in range(H):
                if h % 4 == 0 and h >= 8:
                    pe.wait_ge(lbe, h // 4 - 1)
                ins = pe.transpose(bank(3 + h // 4 % 2, h % 4 * P, (h % 4 + 1) * P),
                                   lf[:, :].rearrange("p (r h) -> p r h", h=H)[:, :, h], ident[:, :])
                if h % 4 == 3:
                    ins.then_inc(lbt, 1)

            s1, s3, s6, s7, s9, ql, tl, te, ex, pn, pl, oa, se = ctr(
                sa1, sa3, sa6, sa7, sa9, qkv_l, tkl, tke, exd, pnd, ptl, oad, seld)
            vi = [Count(vin[n], 16) for n in range(VSLOT)]
            so = Count(so1)

            def sample_max():
                pe.wait_ge(sa1, s1.up())
                pe.transpose(PS[0:H, 7 * BANK + S_MAX:7 * BANK + S_MAX + P], zmax[:, :], ident[:, :]).then_inc(sa2, 1)

            def sample_spread():
                pe.wait_ge(sa3, s3.up())
                pe.matmul(bank(7, S_SPREAD, S_SPREAD + H), ones[0:H, :], mdiag[:, :], start=True, stop=True)\
                  .then_inc(sa4, 1)

            def quadrant(j, a, b):
                return PS[32 * j:32 * j + HQ, 7 * BANK + a:7 * BANK + b]

            def sample_sum():
                pe.wait_ge(sa7, s7.up())
                for j in range(4):
                    ins = pe.matmul(quadrant(j, S_SUM, S_SUM + 1), psum_s[:, HQ * j:HQ * (j + 1)], ones[:, 0:1],
                                    start=True, stop=True)
                ins.then_inc(sa8, 1)

            def value_page(g):
                pe.wait_ge(vin[g % VSLOT], vi[g % VSLOT].up())
                page_product(g, vpage[:, g % VSLOT, :])

            def page_product(g, page):
                for j in range(4):
                    ins = pe.matmul(quadrant(j, S_OUT, S_OUT + 256), ps[:, g, HQ * j:HQ * (j + 1)],
                                    page[:, 256 * j:256 * (j + 1)], start=g == 0, stop=False)
                ins.then_inc(vfr, 1)

            def value_new():
                for j in range(4):
                    pe.matmul(quadrant(j, S_OUT, S_OUT + 256), ps[0:NSEQ, NPG, HQ * j:HQ * (j + 1)],
                              v_s[:, 256 * j:256 * (j + 1)], start=False, stop=True)

            def sample_turn():
                pe.wait_ge(so1, so.up())
                for c in range(2):
                    ins = pe.transpose(bank(7, S_OUT + c * P, S_OUT + (c + 1) * P), o_rows[:, c * P:(c + 1) * P],
                                       ident[:, :])
                ins.then_inc(so2, 1)

            def rows(h):
                return slice(h * DH, (h + 1) * DH)

            def scores(h, t):
                base = 2 * (t % 2) * BANK
                r = rows(h)
                width = max(256, P * (t + 1))
                spans = [(0, min(BANK, width))] + ([(BANK, max(BANK + 256, width))] if width > BANK else [])
                q = slice(t * P, (t + 1) * P)
                for a, b in spans:
                    out = PS[:, base + a:base + b]
                    diagonal = a <= t * P < b
                    pe.matmul(out, q_hi[r, q], k_hi[r, a:b], start=True, stop=False)
                    pe.matmul(out, q_lo[r, q], k_hi[r, a:b], start=False, stop=False)
                    pe.matmul(out, q_hi[r, q], k_lo[r, a:b], start=False, stop=False)
                    ins = pe.matmul(out, sel[h][r, :], negcum[r, a:b], start=False, stop=not diagonal)
                    if diagonal:
                        ins = pe.matmul(PS[:, base + t * P:base + (t + 1) * P], ident_b[:, :], mask_b[:, :],
                                        start=False, stop=True)
                ins.then_inc(sd, 1)

            def transpose_group(n, g, slot):
                for k in range(2):
                    for t in range(2):
                        future = g == n % 4 and k > t
                        src = zeros[:, :] if future else probs[(n % 2) * 2 + t][:, (2 * g + k) * P:(2 * g + k + 1) * P]
                        ins = pe.transpose(bank(4 + slot % 2, (2 * k + t) * P, (2 * k + t + 1) * P), src, ident[:, :])
                ins.then_inc(ptd, 1)

            def value_group(h, jj, g, slot, new=False):
                pe.wait_ge(ptl, pl.up())
                if g == 0 and not new:
                    pe.wait_ge(oad, oa.up())
                for k in range(2):
                    kt = 2 * g + k
                    v = v_pack[:, kt, h, :, :].rearrange("p a d -> p (a d)")
                    pe.matmul(PS[:, 6 * BANK:6 * BANK + 256], v, pt_hi[slot % 2][:, 256 * k:256 * (k + 1)],
                              start=kt == 0, stop=False)
                    ins = pe.matmul(PS[:, 6 * BANK:6 * BANK + 256], v, pt_lo[slot % 2][:, 256 * k:256 * (k + 1)],
                                    start=False, stop=kt == 2 * jj + 1)
                ins.then_inc(pvd, 1)

            def transposes(src, n):
                for t in range(4):
                    ins = pe.transpose(bank(4 + n, t * P, (t + 1) * P), src[:, (4 * n + t) * P:(4 * n + t + 1) * P],
                                       ident[:, :])
                ins.then_inc(tkt, 1)

            def pair(first=False, sample=True, last=False):
                if not first:
                    pe.wait_ge(exd, ex.value)
                    pe.wait_ge(ptl, pl.value)
                open_product(1, fresh=first)
                product_steps(1, a_hi, a_lo, range(KT // 2))
                if sample:
                    sample_max()
                product_steps(1, a_hi, a_lo, range(KT // 2, KT))
                open_product(0)
                product_steps(0, a_hi, a_lo, range(KT // 2))
                if sample:
                    sample_spread()
                pe.wait_ge(ev[1], evd[1].value + 1)
                for n in range(2):
                    transposes(k_raw, n)
                product_steps(0, a_hi, a_lo, range(KT // 2, KT))
                if sample:
                    pe.wait_ge(sa6, s6.up())
                    value_page(0)
                    value_page(1)
                pe.wait_ge(qkv_l, ql.up())
                pe.wait_ge(qkv_l, ql.up())
                pe.wait_ge(seld, se.up())
                pe.wait_ge(ev[0], evd[0].value + 1)
                slot = 0
                for n in range(9):
                    def score(t, n=n):
                        if n > 0:
                            pe.wait_ge(exd, ex.up())
                        scores(n // 4, 2 * (n % 4) + t)

                    if n == 1:
                        for m in range(2):
                            pe.wait_ge(tke, te.up())
                            transposes(qv_raw, m)
                    if n < 2:
                        score(0)
                    if 1 < n and sample:
                        value_page(2 * n - 1)
                    if n == 8 and sample:
                        value_new()
                        sample_sum()
                    if n > 0:
                        h, jj = (n - 1) // 4, (n - 1) % 4
                        if n <= 2:
                            pe.wait_ge(tkl, tl.up())
                            pe.wait_ge(tke, te.up())
                        pn.up()
                        pe.wait_ge(pnd, pn.up())
                        for g in range(min(2, jj + 1)):
                            transpose_group(n - 1, g, slot + g)
                    if n < 8:
                        score(1)
                    elif not last:
                        pe.wait_ge(exd, ex.up())
                        pe.wait_ge(exd, ex.up())
                        open_product(0)
                    else:
                        ex.up()
                        ex.up()
                    if n == 1 and sample:
                        value_page(2)
                    if n > 0:
                        for g in range(jj + 1):
                            if n == 8 and not last:
                                product_steps(0, a_hi, a_lo, range(2 * g, 2 * g + 2))
                            if g == min(2, jj) and jj > 0 and n < 7:
                                score(0, n + 1)
                            value_group(h, jj, g, slot + g, first and n == 1)
                            if g + 2 <= jj:
                                transpose_group(n - 1, g + 2, slot + g + 2)
                            if g == 0 and 1 < n < 8 and sample:
                                value_page(2 * n)
                            if jj == 0 and n < 7:
                                score(0, n + 1)
                        slot += jj + 1
                if sample:
                    sample_turn()

            product(0, a_hi, a_lo)
            pe.wait_ge(ready, 1)
            pair(first=True, sample=False)
            with counted_loop(pe, 1, NPAIR - 1, {
                    s1: 1, s3: 1, s6: 1, s7: 1, so: 1, ql: 2, tl: 2, te: 4, ex: 16, pn: 16, pl: 20, oa: 8, se: 1,
                    wlo[0]: 2, wlo[1]: 1, evd[0]: 2, evd[1]: 1, **{vi[n]: 8 for n in range(VSLOT)}}) as i:
                pair()
            pair(last=True)
            sample_max()
            sample_spread()
            pe.wait_ge(sa6, s6.up())
            for g in range(NPG):
                slot, n_slots = last_slot(g)
                pe.wait_ge(lin[g % n_slots], 16 * (g // n_slots + 1))
                page_product(g, slot)
            value_new()
            sample_sum()
            sample_turn()

            bl = Count(blo)

            def out_product(kts):
                product(0, b_hi, b_lo, kts, parts=bl)
                product(1, b_hi, b_lo, kts)
                with counted_loop(pe, 1, KT // 2, {wlo[0]: 1, wlo[1]: 1, evd[0]: 1, evd[1]: 1}) as i:
                    product(0, b_hi, b_lo, kts)
                    product(1, b_hi, b_lo, kts)

            def next_norm():
                pe.wait_ge(ev[1], evd[1].value + 1)
                sum_squares(t2)

            rqc = Count(rq)
            rqc.up()
            rqc.up()

            def first_normed():
                product(0, a_hi, a_lo, parts=lo_parts)
                next_norm()
                pe.wait_ge(rq, rqc.up())
                rqc.up()

            def final_product(kts):
                def to_rows(m):
                    pe.wait_ge(yt, m + 1)
                    if m > 0:
                        pe.wait_ge(yte, m)
                    for t in range(TT):
                        ins = pe.transpose(PS[:, 6 * BANK + t * P:6 * BANK + (t + 1) * P],
                                           (t0, t1)[m % 2][:, t * P:(t + 1) * P], ident[:, :])
                    ins.then_inc(ytt, 1)

                for m in range(KT):
                    product(m % 2, b_hi, b_lo, kts, parts=bl if m == 0 else None)
                    if m > 0:
                        to_rows(m - 1)
                to_rows(KT - 1)
                pe.wait_ge(ysm, 1)
                for m in range(KT):
                    pe.transpose(PS[0:NSEQ, m * P:(m + 1) * P], smp_g[:, m, :], ident[:, :])
                for _ in range(KT):
                    sq.up()
                pe.wait_ge(sqa, sq.value)
                for t in range(TT):
                    pe.matmul(bank(3, t, t + 1), t2[:, t * P:(t + 1) * P], ones[:, 0:1], start=True, stop=True)
                pe.matmul(PS[0:NSEQ, 3 * BANK + TT:3 * BANK + TT + 1], t2[:, S:T], ones[:, 0:1], start=True, stop=True)\
                  .then_inc(yss, 1)

            def ffn(last=False):
                first_normed()
                product(1, a_hi, a_lo)
                for c, n in enumerate(CHUNKS):
                    with counted_loop(pe, 1 if c == 0 else 0, n,
                                      {wlo[0]: 1, wlo[1]: 1, evd[0]: 1, evd[1]: 1}) as j:
                        product(0, a_hi, a_lo)
                        product(1, a_hi, a_lo)
                    if last and c == len(CHUNKS) - 1:
                        final_product(n)
                    else:
                        out_product(n)

            pe.wait_ge(sa9, NSEQ)
            out_product(KT)
            ffn()
            first_normed()
            for r in range(1, 6):
                product(r % 2, a_hi, a_lo)
            with counted_loop(pe, 1, KT // 2, {wlo[0]: 3, wlo[1]: 3, evd[0]: 3, evd[1]: 3}) as i:
                for r in range(6):
                    product(r % 2, a_hi, a_lo)
            pe.wait_ge(cvt, KT)
            for m in range(KT):
                ins = pe.transpose(PS[0:2 + NSEQ, 6 * BANK + m * P:6 * BANK + (m + 1) * P], conv_rows[:, m, :], ident[:, :])
            ins.then_inc(cvp, 1)
            out_product(KT)
            pe.wait_ge(cvc, 2)
            ffn(last=True)

        @block.vector
        def _(dve):
            steps = Count(dv)

            def then(ins):
                ins.then_inc(dv, 1)
                dve.wait_ge(dv, steps.up())

            done = [Count(mm[s]) for s in range(2)]
            ah, rqc, rrc = ctr(ahi, rq, rr)

            def low_normed(m, x, norm):
                dve.wait_ge(ahi, ah.up())
                if isinstance(m, int):
                    out, hi, g = a_lo[:, m, :], a_hi[:, m, :], vecs[:, m, NORMS[norm]:NORMS[norm] + 1]
                else:
                    out = a_lo[:, bass.ds(m, 1), :].rearrange("p a t -> p (a t)")
                    hi = a_hi[:, bass.ds(m, 1), :].rearrange("p a t -> p (a t)")
                    g = vecs[:, bass.ds(m, 1), NORMS[norm]:NORMS[norm] + 1].rearrange("p a o -> p (a o)")
                dve.scalar_tensor_tensor(out=out, in0=x, scalar=g, in1=hi.bitcast(F32), op0=ALU.mult,
                                         op1=ALU.subtract).then_inc(alo, 1)

            def reciprocals():
                rqc.up()
                dve.wait_ge(rq, rqc.up())
                dve.reciprocal(rinv[:, :], rinv[:, :]).then_inc(rr, 1)
                dve.wait_ge(rr, rrc.up())

            def read_out(s, out, scale=1.0):
                dve.wait_ge(mm[s], done[s].up())
                return dve.scalar_tensor_tensor(out=blocks(out), in0=group(s), scalar=scale, in1=blocks(rinv[:, :]),
                                                op0=ALU.mult, op1=ALU.mult)

            dve.wait_ge(vec_t, 1)
            dve.wait_ge(cst, 7)
            dve.tensor_copy(vecs[:, :, :].rearrange("p k r -> p (k r)"), PS[:, 6 * BANK:6 * BANK + 24 * KT])\
               .then_inc(vec_d, 1)
            dve.tensor_copy(ident_b[:, :], ident[:, :])
            dve.tensor_copy(mask_b[:, :], mask_f[:, :])
            dve.wait_ge(rsm, 1)
            dve.reciprocal(small[0:NSEQ, 2:3], small[0:NSEQ, 1:2])
            dve.wait_ge(vec_d, 1)
            alc = Count(alo)
            for m in range(KT + 1):
                if m < KT:
                    dve.wait_ge(ftr, m + 1)
                    if m >= 3:
                        dve.wait_ge(xsp[m % 3], 16 * (m // 3))
                        dve.wait_ge(sqr, m - 2)
                        dve.wait_ge(alo, m - 2)
                    dve.tensor_copy(xf[m % 3][:, :], PS[:, 3 * (m % 2) * BANK:3 * (m % 2) * BANK + T]).then_inc(fev, 1)
                if m > 0:
                    dve.wait_ge(fev, m)
                    low_normed(m - 1, xf[(m - 1) % 3][:, :], "mix0")
            dve.wait_ge(alo, KT)
            dve.tensor_tensor(hs[:, :, :], a_hi[:, :, S:T].bitcast(F32), a_lo[:, :, S:T].bitcast(F32), ALU.add)\
               .then_inc(hsd, 1)
            reciprocals()
            def segment(n):
                dve.wait_ge(smm, n + 1)
                dst = (q_s, k_s, v_s)[n // 4]
                dve.tensor_scalar(dst[:, n % 4 * 256:(n % 4 + 1) * 256],
                                  PS[0:NSEQ, (6 + n % 2) * BANK:(6 + n % 2) * BANK + 256], small[0:NSEQ, 2:3],
                                  QS if n < 4 else 1.0, ALU.mult, ALU.mult).then_inc(sme, 1)

            dve.wait_ge(mm[0], done[0].up())
            dve.scalar_tensor_tensor(out=blocks(gz[:, :]), in0=group(0)[0:H], scalar=1.0, in1=blocks(rinv[0:H, :]),
                                     op0=ALU.mult, op1=ALU.mult).then_inc(ev[0], 1)
            dve.wait_ge(ev[0], 1)
            dve.wait_ge(misc_in, 48)
            dve.tensor_scalar(gz[:, :], gz[:, :], bf_col[:, 0:1], None, ALU.add).then_inc(fz, 1)
            segment(0)
            dve.wait_ge(fa, 1)
            dve.tensor_scalar(gw[:, :], ge[:, :], 1.0, None, ALU.add).then_inc(fz, 1)
            segment(1)
            segment(2)
            dve.wait_ge(fa, 2)
            gln = gd
            dve.wait_ge(sqa, KT)
            then(dve.tensor_scalar(gw[:, :], gw[:, :], 1.0, None, ALU.subtract))
            then(dve.tensor_scalar(sqt[0][0:H, :], gw[:, :], 0.0, None, ALU.is_equal))
            then(dve.tensor_tensor(gw[:, :], gw[:, :], sqt[0][0:H, :], ALU.add))
            segment(3)
            then(dve.reciprocal(gw[:, :], gw[:, :]))
            segment(4)
            segment(5)
            then(dve.tensor_tensor(gw[:, :], gw[:, :], ge[:, :], ALU.mult))
            then(dve.tensor_tensor(gw[:, :], gw[:, :], gln[:, :], ALU.mult))
            then(dve.tensor_tensor(ge[:, :], ge[:, :], sqt[0][0:H, :], ALU.mult))
            segment(6)
            then(dve.tensor_tensor(gw[:, :], gw[:, :], ge[:, :], ALU.add))
            dve.scalar_tensor_tensor(out=gz[:, :], in0=gz[:, :], scalar=0.0, in1=gw[:, :], op0=ALU.min,
                                     op1=ALU.subtract).then_inc(lgt_in, 1)
            dve.wait_ge(lgt_in, 1)
            segment(7)
            then(dve.memset(sqt[0][:, :], 1.0))
            then(dve.tensor_tensor_scan(ge[:, 0:S], sqt[0][0:H, 0:S], gz[:, 0:S], 0.0, ALU.mult, ALU.add))
            then(dve.tensor_scalar(ge[:, 0:S], ge[:, 0:S], -1.0, None, ALU.mult))
            segment(8)
            dve.wait_ge(lgt, 1)
            dve.tensor_copy(lt[:, 0:TT * H], bank(3, 0, TT * H))
            dve.tensor_copy(lt[0:NSEQ, TT * H:(TT + 1) * H], PS[0:NSEQ, 3 * BANK + TT * H:3 * BANK + (TT + 1) * H])\
               .then_inc(lgo, 1)
            dve.wait_ge(lf_in, 16)
            lf3 = lf[:, :].rearrange("p (r h) -> p h r", h=H)
            lc3 = lc[:, :].rearrange("p (r h) -> p h r", h=H)
            for h in range(H):
                ins = dve.tensor_tensor_scan(lc3[:, h, :], sqt[0][:, 0:PAGE], lf3[:, h, :], 0.0, ALU.mult, ALU.add)
            then(ins)
            dve.tensor_copy(tot[:, :], lc[:, (PAGE - 1) * H:PAGE * H]).then_inc(lct, 1)
            segment(9)
            then(dve.tensor_copy(negcum[0:H, :], ge[:, 0:S]))
            then(dve.tensor_tensor(negcum[32:32 + H, :], ge[:, 0:S], negcum[0:H, :].bitcast(F32), ALU.subtract))
            segment(10)
            dve.wait_ge(lco, 1)
            dve.wait_ge(lct, 1)
            then(dve.tensor_copy(tot[:, :], bank(4, 0, H)))
            dve.tensor_tensor(lf[:, :].rearrange("p (r h) -> p r h", h=H),
                              tot[:, :].unsqueeze(1).to_broadcast([P, PAGE, H]),
                              lc[:, :].rearrange("p (r h) -> p r h", h=H), ALU.subtract).then_inc(lcb, 1)
            then(dve.tensor_copy(negcum[64:64 + H, :], negcum[0:H, :].bitcast(F32)))
            then(dve.tensor_copy(negcum[96:96 + H, :], negcum[32:32 + H, :].bitcast(F32)))
            segment(11)
            for n in range(4):
                dve.wait_ge(lbt, n + 1)
                dve.tensor_copy(s_bias[:, 4 * n:4 * n + 4, :].rearrange("p h g -> p (h g)"), bank(3 + n % 2))\
                   .then_inc(lbe, 1)
            then(dve.tensor_tensor(sqs0[0:NSEQ, 0:D], q_s[:, :], k_s[:, :], ALU.mult))
            then(dve.tensor_reduce(snew_row[:, :], sqs0[0:NSEQ, 0:D].rearrange("p (h d) -> p h d", d=DH), X_AXIS, ALU.add))
            then(dve.tensor_scalar(negd[:, :], ident[0:NSEQ, 0:NSEQ], -1.0, -NEG_INF, ALU.add, ALU.mult))
            rows_h = snew_row[:, :].unsqueeze(1).to_broadcast([NSEQ, NSEQ, H])
            cols_b = ident[0:NSEQ, 0:NSEQ].unsqueeze(2).to_broadcast([NSEQ, NSEQ, H])
            neg_b = negd[:, :].unsqueeze(2).to_broadcast([NSEQ, NSEQ, H])
            then(dve.tensor_tensor(s_new[0:NSEQ, :, :], rows_h, cols_b, ALU.mult))
            then(dve.tensor_tensor(s_new[0:NSEQ, :, :], s_new[0:NSEQ, :, :], neg_b, ALU.add))
            dve.wait_ge(lbe, 4)
            dve.wait_ge(w_lod[0], 1)
            dve.wait_ge(sqa, KT)
            dve.wait_ge(out0, 64)
            dve.wait_ge(qsp, 16)
            dve.nop().then_inc(ready, 1)

            qh, ex, pt, oc, kf, km, s2, s4, s6, s8, s9, te = ctr(
                qkv_h, exd, pth, ocp, kfr, kml, sa2, sa4, sa6, sa8, so2, tke)
            dve.memset(bank(7), 1.0)
            kp = [Count(kin[n], 16) for n in range(KSLOT)]
            qb = Count(qbi, 16)
            ow = Count(osp, 16)
            sdc, pvc = ctr(sd, pvd)
            plc, pnc, mxc = ctr(ptl, pnd, mxd)

            def key_page(g, first):
                slot = kpage[:, g % KSLOT, :]
                dve.wait_ge(kin[g % KSLOT], kp[g % KSLOT].up())
                if g == 0:
                    dve.wait_ge(qbi, qb.up())
                if g in POOL_K:
                    dve.wait_ge(kml, km.up())
                else:
                    then(dve.tensor_tensor(slot, slot, q_bc[:, :], ALU.mult))
                dve.tensor_reduce(s_raw[:, g, :], slot.rearrange("p (h d) -> p h d", d=DH), X_AXIS, ALU.add)\
                   .then_inc(kfr, 1)
                kf.up()

            def sample_scores(b):
                dve.wait_ge(kfr, kf.value)
                bias = s_bias[:, :, bass.ds(b * NPG, NPG)].rearrange("p h g -> p g h")
                dve.tensor_tensor(z[:, 0:NPG, :], s_raw[:, :, :], bias, ALU.add)
                new = s_new[:, bass.ds(b, 1), :]
                then(dve.tensor_copy(z[:, NPG:NPG + 1, :], new))
                dve.tensor_reduce(zmax[:, :], z[:, :, :].rearrange("p g h -> p h g"), X_AXIS, ALU.max).then_inc(sa1, 1)

            def sample_maxima():
                dve.wait_ge(sa2, s2.up())
                then(dve.tensor_reduce(mcol[:, :], PS[0:H, 7 * BANK + S_MAX:7 * BANK + S_MAX + P], X_AXIS, ALU.max))
                dve.tensor_scalar(mdiag[:, :], ident[0:H, 0:H], mcol[:, 0:1], None, ALU.mult).then_inc(sa3, 1)

            def sample_shift():
                dve.wait_ge(sa4, s4.up())
                dve.tensor_tensor(z[:, :, :], z[:, :, :], bank(7, S_SPREAD, S_SPREAD + H).unsqueeze(1).to_broadcast([P, NPG + 1, H]),
                                  ALU.subtract).then_inc(sa5, 1)

            def sample_sums():
                dve.wait_ge(sa6, s6.up())
                dve.tensor_reduce(psum_s[:, :], ps[:, :, :].rearrange("p g h -> p h g"), X_AXIS, ALU.add).then_inc(sa7, 1)

            def sample_scale():
                dve.wait_ge(sa8, s8.up())
                then(dve.reciprocal(rl[:, :], bank(7, S_SUM, S_SUM + 1)))
                dve.tensor_scalar(o_rows[:, :], bank(7, S_OUT, S_OUT + 256), rl[:, 0:1], None, ALU.mult).then_inc(so1, 1)

            def sample_output(b):
                dve.wait_ge(so2, s9.up())
                for c in range(2):
                    for e in range(2):
                        r = slice(e * DH, (e + 1) * DH)
                        src = bank(7, S_OUT + c * P, S_OUT + (c + 1) * P).rearrange("p (j n) -> p j n", n=32)
                        dst = o_smp[:, :, bass.ds(b, 1)].rearrange("p (j c) b -> p j (c b)", c=2)
                        ins = dve.tensor_copy(dst[r, :, c:c + 1], src[r, :, 2 * c + e:2 * c + e + 1])
                ins.then_inc(sa9, 1)

            def pair(i, first=False, sample=True):
                if sample:
                    sample_scores(i - 1)
                dve.wait_ge(qkv_l, qlc.value) if not first else None
                read_out(0, qv_raw[:, :], QS).then_inc(ev[0], 1)
                evc[0].up()
                dve.wait_ge(ev[0], evc[0].value)
                dve.wait_ge(qkv_h, qh.up())
                dve.tensor_tensor(q_lo[:, :], qv_raw[:, 0:S], q_hi[:, :].bitcast(F32), ALU.subtract).then_inc(qkv_l, 1)
                qlc.up()
                for h in range(2):
                    r = slice(h * DH, (h + 1) * DH)
                    ins = dve.tensor_scalar(sel[h][r, :], ones[r, :], sel_col(i, h)[r, :], None, ALU.mult)
                ins.then_inc(seld, 1)
                for g in range(4):
                    key_page(g, first)
                if sample:
                    sample_maxima()
                read_out(1, k_raw[:, :]).then_inc(ev[1], 1)
                evc[1].up()
                dve.wait_ge(ev[1], evc[1].value)
                dve.wait_ge(qkv_h, qh.up())
                dve.tensor_tensor(k_lo[:, :], k_raw[:, 0:S], k_hi[:, :].bitcast(F32), ALU.subtract).then_inc(qkv_l, 1)
                qlc.up()
                for g in (4, 5):
                    key_page(g, first)
                if sample:
                    sample_shift()
                key_page(6, first)
                dve.wait_ge(qkv_l, qlc.value)
                read_out(0, qv_raw[:, :]).then_inc(ev[0], 1)
                evc[0].up()
                key_page(7, first)
                slot = [0]

                def low_v():
                    te.up()
                    te.up()
                    for n in range(2):
                        dve.wait_ge(tke, te.up())
                        dve.tensor_tensor(v_pack[:, 4 * n:4 * n + 4, :, 1, :],
                                          bank(4 + n).rearrange("p (t h c) -> p t h c", h=2, c=DH),
                                          v_pack[:, 4 * n:4 * n + 4, :, 0, :].bitcast(F32), ALU.subtract).then_inc(tkl, 1)

                def maxima(n, t):
                    h, jj = n // 4, n % 4
                    t += 2 * jj
                    dve.wait_ge(sd, sdc.up())
                    base = 2 * (t % 2) * BANK
                    dve.tensor_reduce(nmax[:, 8 * h + t:8 * h + t + 1], PS[:, base:base + P * (t + 1)], X_AXIS,
                                      ALU.max, negate=True).then_inc(mxd, 1)

                def low_transposed(g, n):
                    dve.wait_ge(pth, pt.up())
                    if not (first and n <= 2 and g == 0):
                        dve.wait_ge(pvd, pvc.up())
                    dve.tensor_tensor(pt_lo[slot[0] % 2][:, :], bank(4 + slot[0] % 2),
                                      pt_hi[slot[0] % 2][:, :].bitcast(F32), ALU.subtract).then_inc(ptl, 1)
                    slot[0] += 1

                def output_sum(n):
                    h, jj = n // 4, n % 4
                    dve.wait_ge(ocp, oc.up())
                    if n == 0 and not first:
                        dve.wait_ge(osp, ow.up())
                    r = slice(h * DH, (h + 1) * DH)
                    dve.tensor_tensor(o_pair[r, 256 * jj:256 * (jj + 1)], PS[r, 6 * BANK:6 * BANK + 256],
                                      o_tmp[r, :], ALU.add).then_inc(oad, 1)

                def normalised(n, t):
                    h, jj = n // 4, n % 4
                    t += 2 * jj
                    k = 8 * h + t
                    dve.wait_ge(exd, ex.up())
                    then(dve.reciprocal(lsum[:, k:k + 1], lsum[:, k:k + 1]))
                    pr = probs[(n % 2) * 2 + t % 2][:, 0:P * (t + 1)]
                    dve.tensor_scalar(pr, pr, lsum[:, k:k + 1], None, ALU.mult).then_inc(pnd, 1)

                for n in range(10):
                    if n == 1:
                        low_v()
                    if n < 8:
                        maxima(n, 0)
                    if 2 <= n < 8:
                        key_page(KEYS_IN_PROJECTION + n, first)
                    if n >= 2:
                        output_sum(n - 2)
                    groups = (n - 1) % 4 + 1 if 0 < n < 9 else 0
                    for g in range(min(2, groups)):
                        low_transposed(g, n)
                    if n == 0:
                        maxima(n, 1)
                        normalised(n, 0)
                    elif n < 8:
                        normalised(n, 0)
                        maxima(n, 1)
                        if n == 1:
                            key_page(KEYS_IN_PROJECTION, first)
                            if sample:
                                sample_sums()
                    elif n == 8 and sample:
                        sample_scale()
                    if groups > 2:
                        low_transposed(2, n)
                    if n < 8:
                        normalised(n, 1)
                    if n == 1:
                        key_page(KEYS_IN_PROJECTION + 1, first)
                    if groups > 3:
                        low_transposed(3, n)
                if sample:
                    sample_output(i - 1)

            def sel_col(i, h):
                return sel_id[:, bass.ds(2 * i + h, 1)]

            qlc = Count(qkv_l)
            evc = [Count(ev[s]) for s in range(2)]
            evc[0].value = 1
            pair(0, first=True, sample=False)
            with counted_loop(dve, 1, NPAIR, {
                    qh: 2, ex: 16, pt: 20, oc: 8, kf: 16, km: len(POOL_K), s2: 1, s4: 1, s6: 1, s8: 1, s9: 1, te: 4, qb: 1,
                    ow: 1, sdc: 16, pvc: 20, qlc: 2, evc[0]: 2, evc[1]: 1, done[0]: 2, done[1]: 1,
                    steps: NPG - len(POOL_K) + 16 + 3, **{kp[n]: 4 for n in range(KSLOT)}}) as i:
                pair(i)
            sample_scores(NSEQ - 1)
            sample_maxima()
            sample_shift()
            sample_sums()
            sample_scale()
            sample_output(NSEQ - 1)

            bh = Count(bhi)
            dve.wait_ge(sa9, NSEQ)
            for m in range(KT + 1):
                if m < KT:
                    if m >= 4:
                        dve.wait_ge(blo, m - 3)
                    dve.wait_ge(oin[m % 4], 16 * (m // 4 + 1))
                    dve.tensor_copy((t0, t1, t2, t3)[m % 4][:, S:T], o_smp[:, m, :]).then_inc(oas, 1)
                if m > 0:
                    dve.wait_ge(oas, m)
                    dve.wait_ge(bhi, bh.up())
                    dve.tensor_tensor(b_lo[:, m - 1, :], (t0, t1, t2, t3)[(m - 1) % 4][:, 0:T],
                                      b_hi[:, m - 1, :].bitcast(F32), ALU.subtract).then_inc(blo, 1)
            dve.wait_ge(blo, KT)
            dve.wait_ge(xin, 16)
            bl = Count(blo)
            bl.value = KT

            def tile(t, m):
                return t[:, bass.ds(m, 1), :].rearrange("p a t -> p (a t)")

            def final_adds():
                g = NORMS["final"]
                for m in range(KT):
                    s = m % 2
                    dve.wait_ge(mm[s], done[s].up())
                    dve.tensor_tensor(blocks(x_res[:, m, :]), group(s), blocks(x_res[:, m, :]), ALU.add).then_inc(ev[s], 1)
                    dve.wait_ge(ev[s], evc[s].up())
                    if m >= 2:
                        dve.wait_ge(ytt, m - 1)
                    dve.tensor_scalar((t0, t1)[m % 2][:, :], x_res[:, m, :], vecs[:, m, g:g + 1], None, ALU.mult)\
                       .then_inc(yt, 1)
                dve.tensor_tensor(smp_g[:, :, :], x_res[:, :, S:T], vecs[:, :, g:g + 1].to_broadcast([P, KT, NSEQ]),
                                  ALU.mult).then_inc(ysm, 1)
                dve.wait_ge(yrt, 1)
                dve.reciprocal(r_col[:, 0:TT], r_col[:, 0:TT])
                dve.reciprocal(r_col[0:NSEQ, TT:TT + 1], r_col[0:NSEQ, TT:TT + 1]).then_inc(yrc, 1)
                dve.wait_ge(yrc, 1)
                dve.wait_ge(yte, KT)
                for t in range(0, TT, 2):
                    dve.tensor_scalar(y_tok[:, t, :], y_tok[:, t, :], r_col[:, t:t + 1], None, ALU.mult).then_inc(yrv, 1)
                dve.tensor_scalar(y_smp[:, :], PS[0:NSEQ, 0:D], r_col[0:NSEQ, TT:TT + 1], None, ALU.mult).then_inc(yrv, 1)

            def out_adds(norm=None):
                per = {done[0]: 1, done[1]: 1, evc[0]: 1, evc[1]: 1}
                if norm:
                    per[ah] = 2
                with counted_loop(dve, 0, KT // 2, per) as i:
                    for s in range(2):
                        x = tile(x_res, 2 * i + s)
                        dve.wait_ge(mm[s], done[s].up())
                        dve.tensor_tensor(blocks(x), group(s), blocks(x), ALU.add).then_inc(ev[s], 1)
                        dve.wait_ge(ev[s], evc[s].up())
                        if norm:
                            low_normed(2 * i + s, x, norm)
                if norm:
                    reciprocals()

            sl = Count(sil)
            prc = Count(prd)

            def ffn(norm):
                for c, n in enumerate(CHUNKS):
                    with counted_loop(dve, 0, n, {done[0]: 1, done[1]: 1, evc[0]: 1, evc[1]: 1, sl: 1, prc: 1,
                                                  bl: 1}) as j:
                        dve.wait_ge(blo, bl.value)
                        read_out(0, t0[:, :]).then_inc(ev[0], 1)
                        evc[0].up()
                        read_out(1, t1[:, :]).then_inc(ev[1], 1)
                        dve.wait_ge(ev[1], evc[1].up())
                        dve.wait_ge(sil, sl.up())
                        dve.tensor_tensor(t1[:, :], t1[:, :], t0[:, :], ALU.mult).then_inc(prd, 1)
                        prc.up()
                        bl.up()
                    if norm == "final" and c == len(CHUNKS) - 1:
                        final_adds()
                    else:
                        out_adds(norm if c == len(CHUNKS) - 1 else None)

            out_adds("ffn0")
            ffn("mix1")

            then(dve.memset(t2[:, 0:2], 0.0))
            bh.value = bh.value + HID
            with counted_loop(dve, 0, KT // 2, {done[0]: 3, done[1]: 3, evc[0]: 3, evc[1]: 3, prc: 2, bh: 2, bl: 2,
                                                steps: 2 * 6}) as i:
                for m in range(2):
                    f = 2 * i + m

                    def vec(a, b=None, f=f):
                        return vecs[:, bass.ds(f, 1), a:b or a + 1].rearrange("p a o -> p (a o)")

                    dve.wait_ge(blo, bl.value)
                    read_out(m, t0[:, :]).then_inc(ev[m], 1)
                    evc[m].up()
                    read_out(1 - m, t1[:, :]).then_inc(ev[1 - m], 1)
                    evc[1 - m].up()
                    read_out(m, t2[:, 2:T + 2]).then_inc(ev[m], 1)
                    dve.wait_ge(ev[m], evc[m].up())
                    dve.wait_ge(ev[1 - m], evc[1 - m].value)
                    then(dve.tensor_tensor(t2[:, 2:T + 2], t2[:, 2:T + 2], t1[:, :], ALU.mult))
                    dve.tensor_copy(conv_rows[:, bass.ds(f, 1), :].rearrange("p a r -> p (a r)"), t2[:, S:T + 2])\
                       .then_inc(cvt, 1)
                    then(dve.tensor_scalar(t3[:, :], t2[:, 2:T + 2], vec(TAP + 2), None, ALU.mult))
                    then(dve.scalar_tensor_tensor(out=t3[:, 0:S], in0=t2[:, 1:S + 1], scalar=vec(TAP + 1),
                                                  in1=t3[:, 0:S], op0=ALU.mult, op1=ALU.add))
                    then(dve.scalar_tensor_tensor(out=t3[:, 0:S], in0=t2[:, 0:S], scalar=vec(TAP),
                                                  in1=t3[:, 0:S], op0=ALU.mult, op1=ALU.add))
                    for j in (1, 0):
                        prev = vec(PREV, 24).rearrange("p (b j) -> p b j", j=2)[:, :, j]
                        then(dve.scalar_tensor_tensor(out=t3[:, S:T], in0=prev, scalar=vec(TAP + j),
                                                      in1=t3[:, S:T], op0=ALU.mult, op1=ALU.add))
                    dve.tensor_tensor(t3[:, :], t3[:, :], t0[:, :], ALU.mult).then_inc(prd, 1)
                    dve.wait_ge(prd, prc.up())
                    dve.wait_ge(bhi, bh.up())
                    dve.tensor_tensor(tile(b_lo, f), t3[:, :], tile(b_hi, f).bitcast(F32), ALU.subtract).then_inc(blo, 1)
                    bl.up()
            out_adds("ffn1")
            ffn("final")


_INS = ["x_prompt", "x_sample", "cache_k", "cache_v", "cache_logf", "state_conv", "page_table",
        "norm_mix", "norm_ffn", "w_ffn_in", "w_ffn_out", "norm_final",
        "attn_w_qkvf", "attn_b_f", "attn_w_o", "conv_w_in", "conv_kernel", "conv_w_out"]


def kernel(**inputs):
    import numpy as _np
    import concourse.bacc as _bacc
    from concourse.bass_utils import run_bass_kernel_spmd as _run

    nc = _bacc.Bacc("TRN2", target_bir_lowering=False, num_devices=1, dynamic_dma_scratch_size=4096)
    arrays, args = {}, []
    for name in _INS:
        a = _np.ascontiguousarray(inputs[name])
        arrays[f"in_{name}"] = a
        args.append(nc.dram_tensor(f"in_{name}", a.shape, mybir.dt.from_np(a.dtype), kind="ExternalInput").ap())
    b, s, d = inputs["x_prompt"].shape
    db, ds, _ = inputs["x_sample"].shape
    la, _, _, h, dh = inputs["cache_k"].shape
    lc, _, w1, _ = inputs["state_conv"].shape
    outs = [(b, s, d), (db, ds, d), (la, b, s, h, dh), (la, b, s, h, dh), (la, b, s, h),
            (la, db, ds, h, dh), (la, db, ds, h, dh), (la, db, ds, h), (lc, b, w1, d), (lc, db, w1, d)]
    for i, shape in enumerate(outs):
        args.append(nc.dram_tensor(f"out_{i}", shape, F32, kind="ExternalOutput").ap())
    fox_shortconv_hybrid_step(nc, *args)
    r = _run(nc, [arrays], core_ids=[0])
    return tuple(r.results[0][f"out_{i}"] for i in range(len(outs)))
```
